# Optimizing a Trainium2 kernel written in Bass

```python
import math
import jax, jax.numpy as jnp
from jax import lax
import numpy as np

D_MODEL = 2048
BATCH = 1
SEQ = 256
DEPTH = 2

CHUNK = 64
N_A_LAYERS = DEPTH // 2
N_B_LAYERS = DEPTH - N_A_LAYERS
D_FF = 4 * D_MODEL

SSM_EXPAND = 2
D_INNER = SSM_EXPAND * D_MODEL
SSM_HEAD_DIM = 64
SSM_HEADS = D_INNER // SSM_HEAD_DIM
SSM_GROUPS = 8
SSM_STATE = 128
SSM_CONV = 4
CONV_DIM = D_INNER + 2 * SSM_GROUPS * SSM_STATE
IN_PROJ_DIM = 2 * D_INNER + 2 * SSM_GROUPS * SSM_STATE + SSM_HEADS

DIFF_HEAD_DIM = 128
DIFF_HEADS = D_MODEL // (2 * DIFF_HEAD_DIM)
DIFF_V_DIM = 2 * DIFF_HEAD_DIM
Q_BLOCK = 128
EPS = 1e-5

kernel_name = "yoco_mamba2_diff_attn_trunk"

def rms_norm(x, w):
    xf = x.astype(jnp.float32)
    xf = xf * lax.rsqrt(jnp.mean(xf * xf, axis=-1, keepdims=True) + EPS)
    return (xf * w.astype(jnp.float32)).astype(x.dtype)

def gated_group_rms_norm(y, z, w):
    g = (y * jax.nn.silu(z)).astype(jnp.float32)
    shp = g.shape
    g = g.reshape(shp[:-1] + (SSM_GROUPS, D_INNER // SSM_GROUPS))
    g = g * lax.rsqrt(jnp.mean(g * g, axis=-1, keepdims=True) + EPS)
    return (g.reshape(shp) * w.astype(jnp.float32)).astype(y.dtype)

def causal_depthwise_conv(x, w, b):
    out = lax.conv_general_dilated(
        x, w[:, None, :].astype(x.dtype), window_strides=(1,), padding=[(SSM_CONV - 1, 0)],
        dimension_numbers=("NWC", "WIO", "NWC"), feature_group_count=x.shape[-1])
    return out + b.astype(x.dtype)

def ssd_scan(x, da, bm, cm):
    out_dtype = x.dtype
    b, s, h, p = x.shape
    g, n = bm.shape[2], bm.shape[3]
    r = h // g
    nc = s // CHUNK
    xc = x.astype(jnp.float32).reshape(b, nc, CHUNK, g, r, p)
    ac = da.astype(jnp.float32).reshape(b, nc, CHUNK, g, r)
    bc = bm.astype(jnp.float32).reshape(b, nc, CHUNK, g, n)
    cc = cm.astype(jnp.float32).reshape(b, nc, CHUNK, g, n)
    a_cs = jnp.cumsum(ac, axis=2)
    seg = a_cs[:, :, :, None] - a_cs[:, :, None, :]
    tri = jnp.tril(jnp.ones((CHUNK, CHUNK), dtype=bool))[None, None, :, :, None, None]
    decay = jnp.exp(jnp.where(tri, seg, -jnp.inf))
    cb = jnp.einsum('bclgn,bcsgn->bclsg', cc, bc)
    y_diag = jnp.einsum('bclsg,bclsgr,bcsgrp->bclgrp', cb, decay, xc)
    decay_to_end = jnp.exp(a_cs[:, :, -1:] - a_cs)
    states = jnp.einsum('bclgn,bclgr,bclgrp->bcgrpn', bc, decay_to_end, xc)
    chunk_decay = jnp.exp(a_cs[:, :, -1])

    def step(carry, inp):
        st, dec = inp
        new = carry * dec[..., None, None] + st
        return new, carry

    init = jnp.zeros((b, g, r, p, n), jnp.float32)
    _, prev = lax.scan(step, init, (jnp.moveaxis(states, 1, 0), jnp.moveaxis(chunk_decay, 1, 0)))
    prev = jnp.moveaxis(prev, 0, 1)
    y_off = jnp.einsum('bclgn,bcgrpn,bclgr->bclgrp', cc, prev, jnp.exp(a_cs))
    return (y_diag + y_off).reshape(b, s, h, p).astype(out_dtype)

def mamba2_mixer(h, w_in, conv_w, conv_b, dt_bias, a_log, d_skip, out_norm_w, w_out):
    b, s, _ = h.shape
    zxbcdt = h @ w_in
    z = zxbcdt[..., :D_INNER]
    xbc = zxbcdt[..., D_INNER:D_INNER + CONV_DIM]
    dt = zxbcdt[..., D_INNER + CONV_DIM:]
    xbc = jax.nn.silu(causal_depthwise_conv(xbc, conv_w, conv_b))
    xs = xbc[..., :D_INNER].reshape(b, s, SSM_HEADS, SSM_HEAD_DIM)
    bm = xbc[..., D_INNER:D_INNER + SSM_GROUPS * SSM_STATE].reshape(b, s, SSM_GROUPS, SSM_STATE)
    cm = xbc[..., D_INNER + SSM_GROUPS * SSM_STATE:].reshape(b, s, SSM_GROUPS, SSM_STATE)
    dt = jax.nn.softplus((dt + dt_bias).astype(jnp.float32))
    a = -jnp.exp(a_log.astype(jnp.float32))
    y = ssd_scan(xs * dt[..., None].astype(xs.dtype), dt * a, bm, cm)
    y = y + xs * d_skip[:, None].astype(xs.dtype)
    y = gated_group_rms_norm(y.reshape(b, s, D_INNER), z, out_norm_w)
    return y @ w_out

def shared_kv(h, kv_norm_w, w_kv, k_norm_w):
    b, s, _ = h.shape
    kv = rms_norm(h, kv_norm_w) @ w_kv
    k = rms_norm(kv[..., :D_MODEL].reshape(b, s, DIFF_HEADS, 2, DIFF_HEAD_DIM), k_norm_w)
    v = kv[..., D_MODEL:].reshape(b, s, DIFF_HEADS, DIFF_V_DIM)
    return k, v

def diff_attention(h, k, v, w_q, q_norm_w, lam_q1, lam_k1, lam_q2, lam_k2, subln_w, w_o, lambda_init):
    b, s, _ = h.shape
    q = rms_norm((h @ w_q).reshape(b, s, DIFF_HEADS, 2, DIFF_HEAD_DIM), q_norm_w)
    lam = (jnp.exp(jnp.sum(lam_q1.astype(jnp.float32) * lam_k1.astype(jnp.float32)))
           - jnp.exp(jnp.sum(lam_q2.astype(jnp.float32) * lam_k2.astype(jnp.float32)))
           + lambda_init)
    scale = DIFF_HEAD_DIM ** -0.5
    nqb = s // Q_BLOCK
    qb = jnp.moveaxis(q.reshape(b, nqb, Q_BLOCK, DIFF_HEADS, 2, DIFF_HEAD_DIM), 1, 0)
    key_chunk = jnp.arange(s) // CHUNK

    def block(args):
        qblk, i = args
        sc = jnp.einsum('bqhcd,bkhcd->bhcqk', qblk, k).astype(jnp.float32) * scale
        q_chunk = (i * Q_BLOCK + jnp.arange(Q_BLOCK)) // CHUNK
        mask = key_chunk[None, :] <= q_chunk[:, None]
        sc = jnp.where(mask[None, None, None], sc, -jnp.inf)
        pr = jax.nn.softmax(sc, axis=-1).astype(v.dtype)
        o = jnp.einsum('bhcqk,bkhv->bhcqv', pr, v)
        o = o[:, :, 0].astype(jnp.float32) - lam * o[:, :, 1].astype(jnp.float32)
        return jnp.transpose(o, (0, 2, 1, 3)).astype(h.dtype)

    o = lax.map(block, (qb, jnp.arange(nqb)))
    o = jnp.moveaxis(o, 0, 1).reshape(b, s, DIFF_HEADS, DIFF_V_DIM)
    o = rms_norm(o, subln_w) * (1.0 - lambda_init)
    return o.reshape(b, s, D_MODEL) @ w_o

def sq_relu_mlp(h, w_up, w_down):
    return jnp.square(jax.nn.relu(h @ w_up)) @ w_down

def setup_inputs(seed: int = 0) -> dict:
    key = jax.random.key(seed)
    ks = jax.random.split(key, 26)
    f32 = jnp.float32

    def nrm(k, shape, scale):
        return jax.random.normal(k, shape, f32) * scale

    def gain(k, shape):
        return 1.0 + 0.02 * jax.random.normal(k, shape, f32)

    u = jax.random.uniform(ks[8], (N_A_LAYERS, SSM_HEADS), f32)
    dt0 = jnp.maximum(jnp.exp(u * (math.log(0.1) - math.log(0.001)) + math.log(0.001)), 1e-4)
    dt_bias = dt0 + jnp.log(-jnp.expm1(-dt0))
    a_log = jnp.log(jax.random.uniform(ks[9], (N_A_LAYERS, SSM_HEADS), f32, 1.0, 16.0))
    return {
        "x": jax.random.normal(ks[0], (BATCH, SEQ, D_MODEL), f32),
        "mlp_norm_w": gain(ks[1], (DEPTH, D_MODEL)),
        "w_up": nrm(ks[2], (DEPTH, D_MODEL, D_FF), D_MODEL ** -0.5),
        "w_down": nrm(ks[3], (DEPTH, D_FF, D_MODEL), D_FF ** -0.5),
        "ssm_norm_w": gain(ks[4], (N_A_LAYERS, D_MODEL)),
        "ssm_w_in": nrm(ks[5], (N_A_LAYERS, D_MODEL, IN_PROJ_DIM), D_MODEL ** -0.5),
        "ssm_conv_w": nrm(ks[6], (N_A_LAYERS, SSM_CONV, CONV_DIM), SSM_CONV ** -0.5),
        "ssm_conv_b": nrm(ks[7], (N_A_LAYERS, CONV_DIM), 0.02),
        "ssm_dt_bias": dt_bias,
        "ssm_a_log": a_log,
        "ssm_d": gain(ks[10], (N_A_LAYERS, SSM_HEADS)),
        "ssm_out_norm_w": gain(ks[11], (N_A_LAYERS, D_INNER)),
        "ssm_w_out": nrm(ks[12], (N_A_LAYERS, D_INNER, D_MODEL), D_INNER ** -0.5),
        "kv_norm_w": gain(ks[13], (D_MODEL,)),
        "w_kv": nrm(ks[14], (D_MODEL, 2 * D_MODEL), D_MODEL ** -0.5),
        "k_norm_w": gain(ks[15], (DIFF_HEAD_DIM,)),
        "attn_norm_w": gain(ks[16], (N_B_LAYERS, D_MODEL)),
        "w_q": nrm(ks[17], (N_B_LAYERS, D_MODEL, D_MODEL), D_MODEL ** -0.5),
        "q_norm_w": gain(ks[18], (N_B_LAYERS, DIFF_HEAD_DIM)),
        "lam_q1": nrm(ks[19], (N_B_LAYERS, DIFF_HEAD_DIM), 0.1),
        "lam_k1": nrm(ks[20], (N_B_LAYERS, DIFF_HEAD_DIM), 0.1),
        "lam_q2": nrm(ks[21], (N_B_LAYERS, DIFF_HEAD_DIM), 0.1),
        "lam_k2": nrm(ks[22], (N_B_LAYERS, DIFF_HEAD_DIM), 0.1),
        "subln_w": gain(ks[23], (N_B_LAYERS, DIFF_V_DIM)),
        "w_o": nrm(ks[24], (N_B_LAYERS, D_MODEL, D_MODEL), D_MODEL ** -0.5),
    }

def reference(x, mlp_norm_w, w_up, w_down, ssm_norm_w, ssm_w_in, ssm_conv_w, ssm_conv_b,
              ssm_dt_bias, ssm_a_log, ssm_d, ssm_out_norm_w, ssm_w_out, kv_norm_w, w_kv,
              k_norm_w, attn_norm_w, w_q, q_norm_w, lam_q1, lam_k1, lam_q2, lam_k2, subln_w, w_o):
    h = x
    k = v = None
    for l in range(DEPTH):
        if l < N_A_LAYERS:
            h = h + mamba2_mixer(rms_norm(h, ssm_norm_w[l]), ssm_w_in[l], ssm_conv_w[l], ssm_conv_b[l],
                                 ssm_dt_bias[l], ssm_a_log[l], ssm_d[l], ssm_out_norm_w[l], ssm_w_out[l])
        else:
            j = l - N_A_LAYERS
            if j == 0:
                k, v = shared_kv(h, kv_norm_w, w_kv, k_norm_w)
            lambda_init = 0.8 - 0.6 * math.exp(-0.3 * l)
            h = h + diff_attention(rms_norm(h, attn_norm_w[j]), k, v, w_q[j], q_norm_w[j],
                                   lam_q1[j], lam_k1[j], lam_q2[j], lam_k2[j], subln_w[j], w_o[j],
                                   lambda_init)
        h = h + sq_relu_mlp(rms_norm(h, mlp_norm_w[l]), w_up[l], w_down[l])
    return h


_drawn_inputs = setup_inputs


def setup_inputs(seed=0):
    import zlib

    import numpy as np

    out = dict(_drawn_inputs(seed))
    spreads = {}
    factors = {'mlp_norm_w': 2.732,
     'ssm_d': 4.763,
     'ssm_out_norm_w': 3.509,
     'kv_norm_w': 6.789,
     'k_norm_w': 8.0,
     'attn_norm_w': 8.0,
     'q_norm_w': 8.0,
     'lam_k1': 2.73,
     'subln_w': 7.95}
    for name, (base, spread) in spreads.items():
        noise = np.random.default_rng([zlib.crc32(name.encode()), seed]).standard_normal(out[name].shape)
        drawn = base * np.exp(spread * noise) if base else spread * noise
        out[name] = __import__('jax').numpy.asarray(drawn.astype(out[name].dtype))
    for name, factor in factors.items():
        out[name] = (out[name] * factor).astype(out[name].dtype)
    return out
```

```python
import math
import numpy as np
import concourse.bass as bass
import concourse.mybir as mybir
from contextlib import ExitStack

F32 = mybir.dt.float32
F32R = mybir.dt.float32r
ALU = mybir.AluOpType
ACT = mybir.ActivationFunctionType
AX = mybir.AxisListType

P = 128
SEQ, D, FF = 256, 2048, 8192
TT = SEQ // P
KT = D // P
NB = 512
INNER, HEADS, HP, GROUPS = 4096, 64, 64, 8
HG = HEADS // GROUPS
GC = INNER // GROUPS
CH = 64
TAPS = 4
CT = (INNER + 2 * GROUPS * P) // P
EPS = 1e-5
HD = 128
LAMBDA_INIT = 0.8 - 0.6 * math.exp(-0.3)
NEG = -1e30

RING = 4
PIECE = 1024

PER_GROUP = 20
IN0 = 1
OUT0 = IN0 + GROUPS * PER_GROUP
UP0 = OUT0 + 4 * 16
PER_CHUNK = 64
ATT0 = UP0 + 4 * PER_CHUNK
PER_PAIR = 24
WO0 = ATT0 + 4 * PER_PAIR
UP1 = WO0 + 4 * 8
PIECES = UP1 + 4 * PER_CHUNK

R_OUT, R_MLP0, R_WO, R_MLP1 = 0, 4, 20, 24
T_OUT, T_MLP0, T_MLP0_END, T_WO, T_MLP1 = 0, 4, 20, 24, 28
ROWS = (2 * CT, 2 * CT, CT, 5 * KT + INNER // P + 4)
ROW_LOADS = 14

WO_ORDER = ([(n, k) for n in (0, 1) for k in range(0, 12, 2)] + [(n, k) for n in (0, 1) for k in (12, 14)]
            + [(n, k) for n in (2, 3) for k in range(0, KT, 2)])

C_CONV, C_CBIAS, C_NORM = 0, TAPS * CT, (TAPS + 1) * CT
N_SSM, N_MLP0, N_MLP1, N_KV, N_ATT, N_OUT = (C_NORM + KT * i for i in range(6))
N_K = N_OUT + INNER // P
N_Q, N_SUB = N_K + 1, N_K + 2
PARAMS = N_SUB + 2


class Pos:

    def __init__(self, c, i=0, m=0):
        self.c, self.i, self.m = c, i, m
        assert m % RING == 0

    def slot(self, off):
        return (self.c + off) % RING

    def done(self, off):
        return self.i * self.m + (self.c + off + 1) if self.m else self.c + off + 1

    def turn(self, off):
        n = (self.c + off) // RING + 1
        return self.i * (self.m // RING) + n if self.m else n


class Chain:

    def __init__(self, eng, sem):
        self.eng, self.sem, self.n, self.base = eng, sem, 0, 0

    def __call__(self, ins):
        ins.then_inc(self.sem, 1)
        self.n += 1
        self.eng.wait_ge(self.sem, self.base + self.n)

    def enter(self, i, first, per):
        self.before = self.n
        self.base, self.n = (i - first) * per + self.before, 0
        self.per = per

    def leave(self, rounds):
        assert self.n == self.per, (self.n, self.per)
        self.base, self.n = 0, self.before + rounds * self.per


def wait(eng, sem, n):
    if not (isinstance(n, int) and n <= 0):
        eng.wait_ge(sem, n)


def col(t, c):
    return t[:, c:c + 1] if isinstance(c, int) else t[:, bass.ds(c, 1)]


def one(c, n):
    return slice(c, c + n) if isinstance(c, int) else bass.ds(c, n)


def one_tile(st, kt, part):
    return st[:, kt, part, :] if isinstance(kt, int) else st[:, bass.ds(kt, 1), part, :].squeeze(1)


def cols3(t, n0, n, c):
    return t[:, n0:n0 + n, one(c, HG)]


def cols(t, c, n):
    return t[:, c:c + n] if isinstance(c, int) else t[:, bass.ds(c, n)]


def trunk(nc, x, mlp_norm_w, w_up, w_down, ssm_norm_w, ssm_w_in, ssm_conv_w, ssm_conv_b, ssm_dt_bias,
          ssm_a_log, ssm_d, ssm_out_norm_w, ssm_w_out, kv_norm_w, w_kv, k_norm_w, attn_norm_w, w_q,
          q_norm_w, lam_q1, lam_k1, lam_q2, lam_k2, subln_w, w_o, out):
    ctx = ExitStack()
    with ctx:
        def sb(name, shape, dt=F32):
            return ctx.enter_context(nc.sbuf_tensor(name, shape, dt))

        sems = {}

        def sem(name):
            if name not in sems:
                sems[name] = ctx.enter_context(nc.semaphore(name))
            return sems[name]

        h = sb("resid", [P, TT, D])
        st = sb("stationary", [P, 3 * KT, 2, SEQ], F32R)
        RA, RB, RC = 0, KT, 2 * KT
        raw = sb("w_raw", [P, RING, PIECE])
        whi = sb("w_hi", [P, RING, PIECE], F32R)
        wlo = sb("w_lo", [P, RING, PIECE], F32R)
        par = sb("params", [P, PARAMS])
        ident = sb("ident", [P, P])
        no_later = sb("no_later", [P, P])
        dt = sb("dt", [P, TT, HEADS])
        dskip = sb("dskip", [P, HEADS])
        colv = sb("colv", [P, 6, HEADS])
        small = sb("small", [P, 64])
        nhalf = small[:, 0:8]
        x_ss, x_rs = small[:, 8:10], small[:, 10:12]
        g_ss, g_ms, g_rs = small[:, 12:14], small[:, 14:16], small[:, 16:18]
        h_ss, h_ms, h_rs = small[:, 18:26], small[:, 26:28], small[:, 28:30]
        kq_ss, kq_rs = small[:, 30:38], small[:, 38:46]
        coef = small[:, 46:54]
        o_ss, o_rs = small[:, 54:58], small[:, 58:62]
        lam_s = small[:, 62:64]
        arena = sb("work", [P, 10112])

        at = [0]

        def view(n, reset=None):
            if reset is not None:
                at[0] = reset
            v = arena[:, at[0]:at[0] + n]
            at[0] += n
            assert at[0] <= 10112
            return v

        zg = view(1024, 0).rearrange("p (t c) -> p t c", t=TT)
        xraw = view(1024).rearrange("p (t c) -> p t c", t=TT)
        bcraw = view(512).rearrange("p (t c) -> p t c", t=TT)
        bct = view(512).rearrange("p (i t) -> p i t", i=2)
        cvx = view(1024).rearrange("p (i t) -> p i t", i=4)
        th = view(512).rearrange("p (i t) -> p i t", i=2)
        gbuf = view(1024).rearrange("p (t c) -> p t c", t=TT)
        xdt = view(1024).rearrange("p (t c) -> p t c", t=TT)
        m0 = view(2048).rearrange("p (h l) -> p h l", h=HG)
        m1 = view(1024).rearrange("p (h l) -> p h l", h=HG)
        cb = view(384)
        xn = view(4096, 0).rearrange("p (t c) -> p t c", t=TT)
        prow = view(4 * P, 5120).rearrange("p (r c) -> p r c", r=4)
        dts = view(8 * 128).rearrange("p (n c) -> p n c", n=8)
        rowsb = view(SEQ)
        kmat = view(5 * P).rearrange("p (n c) -> p n c", n=5)
        da = view(TT * HEADS).rearrange("p (t c) -> p t c", t=TT)
        dtb = view(HEADS)
        alog = view(HEADS)
        lamv = view(4 * P, 8704).rearrange("p (n c) -> p n c", n=4)
        lamt = view(2 * P).rearrange("p (n c) -> p n c", n=2)
        act = view(1024, 0).rearrange("p (t c) -> p t c", t=TT)
        pt = arena[:, 0:768].rearrange("p (h q) -> p h q", h=2)
        s0 = view(512).rearrange("p (s k) -> p s k", s=4)
        vall = view(TT * D).rearrange("p (t c) -> p t c", t=TT)
        kq = view(1024).rearrange("p (t c) -> p t c", t=TT)
        kT = view(1024).rearrange("p (s t) -> p s t", s=4)
        qT = view(1024).rearrange("p (s t) -> p s t", s=4)
        s1_at = at[0]
        s1 = view(1024).rearrange("p (s k) -> p s k", s=4)
        ob = arena[:, s1_at:s1_at + 1024].rearrange("p (t c) -> p t c", t=TT)
        mask0, mask1 = view(P), view(SEQ)

        acc = [ctx.enter_context(nc.psum_tensor(f"acc{i}", [P, TT, NB], F32)) for i in range(2)]
        aux = [ctx.enter_context(nc.psum_tensor(f"aux{i}", [P, TT, NB], F32)) for i in range(2)]
        rows_dram = nc.dram_tensor("decay_rows", [HEADS, SEQ], F32).ap()

        conv_w = lambda j, ct: col(par, ct + (C_CONV + j * CT))
        conv_b = lambda ct: col(par, ct + C_CBIAS)
        param = lambda c: col(par, c)

        def to_channels(bank):
            return lambda i, t: bank[:, i // 2, (i % 2) * SEQ + t * P:(i % 2) * SEQ + (t + 1) * P]

        def turned_tile(bank, i):
            return bank[:, i // 2, (i % 2) * SEQ:(i % 2 + 1) * SEQ]

        def whole(bank):
            return bank[:, :, :].rearrange("p a (b t) -> p (a b) t", t=SEQ)

        block = ctx.enter_context(nc.Block())

        @block.sync
        def _(sp):
            for t in range(TT):
                sp.dma_start(h[:, t, :], x[0, t * P:(t + 1) * P, :]).then_inc(sem("x_in"), 16)

            def load(pos, off, parts):
                wait(sp, sem("lo_made"), pos.done(off) - RING)
                dst = raw[:, pos.slot(off), :].rearrange("p (c k n) -> p c k n", c=len(parts), k=parts[0].shape[1])
                for c, src in enumerate(parts):
                    sp.dma_start(dst[:, c], src).then_inc(sem(f"raw_in{pos.slot(off)}"), 32 // len(parts))

            def blocks(pos, off, w, n0, pieces, k0=0):
                if not isinstance(n0, int):
                    sp.to_reg(n0 * 4)
                for j in range(pieces):
                    load(pos, off + j, (w[:, one(k0 + 2 * j, 2), one(n0, NB)],))

            w_in = ssm_w_in[0].rearrange("(k p) n -> p k n", p=P)
            load(Pos(0), 0, (w_in[:, :, 2 * INNER + 2 * GROUPS * P:],))

            def group(g):
                pos = Pos(IN0, g, PER_GROUP)
                for j in range(4):
                    load(pos, j, [w_in[:, 4 * j:4 * j + 4, one(g * P + (2 * INNER + i * GROUPS * P), P)] for i in range(2)])
                blocks(pos, 4, w_in, g * GC + INNER, 8)
                blocks(pos, 12, w_in, g * GC, 8)

            group(0)
            with sp.Fori(1, GROUPS) as g:
                group(g)

            with sp.Fori(0, 4) as n:
                blocks(Pos(OUT0, n, 16), 0, ssm_w_out[0].rearrange("(k p) n -> p k n", p=P), n * NB, 16)

            def mlp(layer, base):
                up = w_up[layer].rearrange("(k p) n -> p k n", p=P)
                down = w_down[layer].rearrange("(k p) n -> p k n", p=P)
                with sp.Fori(0, 4) as c:
                    with sp.Fori(0, 4) as u:
                        blocks(Pos(base, c * 8 + u, 8), 0, up, c * D + u * NB, 8)
                    with sp.Fori(0, 4) as u:
                        blocks(Pos(base + 32, c * 8 + u, 8), 0, down, u * NB, 8, c * KT)

            mlp(0, UP0)
            kv = w_kv.rearrange("(k p) n -> p k n", p=P)
            wq = w_q[0].rearrange("(k p) n -> p k n", p=P)
            with sp.Fori(0, 4) as j:
                pos = Pos(ATT0, j, PER_PAIR)
                blocks(pos, 0, kv, j * NB + D, 8)
                blocks(pos, 8, kv, j * NB, 8)
                blocks(pos, 16, wq, j * NB, 8)
            wo = w_o[0].rearrange("(k p) n -> p k n", p=P)
            for i, (n, kt) in enumerate(WO_ORDER):
                load(Pos(WO0), i, (wo[:, kt:kt + 2, n * NB:(n + 1) * NB],))
            mlp(1, UP1)

            out_v = out[0].rearrange("(t p) c -> p t c", p=P)
            for n in range(4):
                sp.wait_ge(sem("resid_added"), R_MLP1 + 12 + n + 1)
                sp.dma_start(out_v[:, :, n * NB:(n + 1) * NB], h[:, :, n * NB:(n + 1) * NB]).then_inc(sem("stored"), 16)
            sp.wait_ge(sem("stored"), 4 * 16)

        @block.tensor
        def _(pe):
            def piece(pos, off, ps, ncol, kt, first, last):
                pe.wait_ge(sem("lo_made"), pos.done(off))
                tiles = PIECE // ncol
                hi, lo = (v[:, pos.slot(off), :] for v in (whi, wlo))
                if ncol == 2 * P:
                    hi, lo = (v.rearrange("p (c k n) -> p k c n", c=2, k=tiles) for v in (hi, lo))
                else:
                    hi, lo = (v.rearrange("p (k n) -> p k n", k=tiles) for v in (hi, lo))
                for k in range(tiles):
                    start, stop = first and k == 0, last and k == tiles - 1
                    for t in range(TT):
                        xh, xl = (st[:, kt + k, i, t * P:(t + 1) * P] for i in range(2))
                        o = ps[:, t, 0:ncol]
                        pe.matmul(o, xh, hi[:, k], start=start, stop=False)
                        pe.matmul(o, xh, lo[:, k], start=False, stop=False)
                        mm = pe.matmul(o, xl, hi[:, k], start=False, stop=stop)
                mm.then_inc(sem("w_used"), 1)

            def transposes(dst, src, tiles=4):
                for i in range(tiles):
                    for t in range(TT):
                        tr = pe.transpose(dst(i, t), src(i, t), ident[:, :])
                return tr

            pe.wait_ge(sem("ident_made"), 2)
            pe.wait_ge(sem("rows_in"), 16 * ROW_LOADS)
            c = 0
            for r, n in enumerate(ROWS):
                tr = pe.transpose(acc[0][:, 0, c:c + n], prow[0:n, r, :], ident[0:n, 0:n])
                c += n
            tr.then_inc(sem("par_turned"), 1)
            for i, bank in enumerate((aux[0], aux[1], acc[1], acc[0])):
                if i == 0:
                    pe.wait_ge(sem("xn_made"), 2)
                if i == 3:
                    pe.wait_ge(sem("par_made"), 3)
                transposes(to_channels(bank), lambda c, t: xn[:, t, (4 * i + c) * P:(4 * i + c + 1) * P]).then_inc(sem("x_turned"), 1)

            pe.wait_ge(sem("x_split"), 4)
            piece(Pos(0), 0, aux[0], HEADS, RA, True, True)

            def turn_x_back(r):
                pe.wait_ge(sem("x_conv"), 2 * r + 2)
                transposes(lambda i, t: aux[1][:, t, i * P:(i + 1) * P],
                           lambda i, t: cvx[:, i, t * P:(t + 1) * P]).then_inc(sem("x_back"), 1)

            def scan(r):
                pe.wait_ge(sem("xdt_made"), r + 1)
                pe.wait_ge(sem("m_made"), r + 1)
                for k in range(HG):
                    c = slice(k * HP, (k + 1) * HP)
                    pe.matmul(aux[1][:, 0, c], m0[:, k, 0:P], xdt[:, 0, c], start=True, stop=True)
                    pe.matmul(aux[1][:, 1, c], m0[:, k, P:], xdt[:, 0, c], start=True, stop=False)
                    mm = pe.matmul(aux[1][:, 1, c], m1[:, k, :], xdt[:, 1, c], start=False, stop=True)
                mm.then_inc(sem("y_ready"), 1)

            def turn_gated(r):
                pe.wait_ge(sem("g_normed"), r + 1)
                transposes(to_channels(aux[0]), lambda i, t: gbuf[:, t, i * P:(i + 1) * P]).then_inc(sem("g_turned"), 1)

            def decays():
                pe.wait_ge(sem("kmat_made"), 1)
                pe.wait_ge(sem("da_made"), 1)
                for t in range(TT):
                    pe.matmul(aux[1][0:HEADS, 0, t * P:(t + 1) * P], da[:, t, :], kmat[:, 4, :], start=True, stop=True)
                o = lambda n: aux[1][:, 1, n * HEADS:(n + 1) * HEADS]
                pe.matmul(o(3), kmat[:, 2, :], da[:, 0, :], start=True, stop=False)
                pe.matmul(o(3), kmat[:, 3, :], da[:, 1, :], start=False, stop=True)
                for n, k, t in ((0, 0, 0), (1, 1, 0), (2, 2, 0), (4, 0, 1), (5, 1, 1)):
                    mm = pe.matmul(o(n), kmat[:, k, :], da[:, t, :], start=True, stop=True)
                mm.then_inc(sem("decays_ready"), 1)

            def group(g, first):
                pos = Pos(IN0, g, PER_GROUP)
                for j in range(PER_GROUP):
                    if j == 0:
                        if first:
                            pe.wait_ge(sem("dt_read"), 1)
                        else:
                            wait(pe, sem("gate_lo"), g - 1)
                    if j == 4 and not first:
                        pe.wait_ge(sem("x_read"), g)
                    if j == 12 and not first:
                        pe.wait_ge(sem("z_read"), g)
                    if j < 4:
                        piece(pos, j, aux[0], 2 * P, RA + 4 * j, j == 0, j == 3)
                    elif j < 12:
                        piece(pos, j, acc[0], NB, RA + 2 * (j - 4), j == 4, j == 11)
                    else:
                        piece(pos, j, acc[1], NB, RA + 2 * (j - 12), j == 12, j == 19)
                    if j == 2 and not first:
                        turn_x_back(g - 1)
                    if j == 5 and first:
                        decays()
                    if j == 6:
                        pe.wait_ge(sem("bc_read"), g + 1)
                        transposes(lambda i, t: aux[0][:, 0, i * SEQ + t * P:i * SEQ + (t + 1) * P],
                                   lambda i, t: bcraw[:, t, i * P:(i + 1) * P], 2).then_inc(sem("bc_turned"), 1)
                    if j == 7 and not first:
                        scan(g - 1)
                    if j == 11:
                        pe.wait_ge(sem("bc_conv"), g + 1)
                        b, c = bct[:, 0, :], bct[:, 1, :]
                        pe.matmul(aux[0][:, 1, 0:SEQ], b[:, 0:P], c, start=True, stop=True)
                        pe.matmul(aux[0][:, 1, SEQ:SEQ + P], b[:, P:], c[:, P:], start=True, stop=True).then_inc(sem("cb_ready"), 1)
                    if j == 14:
                        pe.wait_ge(sem("x_read"), g + 1)
                        if first:
                            pe.wait_ge(sem("decays_read"), 1)
                        else:
                            pe.wait_ge(sem("y_read"), g)
                        transposes(to_channels(aux[1]), lambda i, t: xraw[:, t, i * P:(i + 1) * P]).then_inc(sem("x_raw_turned"), 1)
                    if j == 15 and not first:
                        pe.wait_ge(sem("cb_read"), g + 1)
                        turn_gated(g - 1)

            group(0, True)
            with pe.Fori(1, GROUPS) as g:
                group(g, False)

            def turn_resid(n, added, turned):
                pe.wait_ge(sem("resid_added"), added)
                transposes(to_channels(aux[n % 2]), lambda i, t: h[:, t, n * NB + i * P:n * NB + (i + 1) * P]).then_inc(sem("turned"), 1)

            for n in range(4):
                for j in range(16):
                    if n == 0 and j == 0:
                        pe.wait_ge(sem("gate_lo"), GROUPS - 1)
                        pe.wait_ge(sem("x_read"), GROUPS)
                    if n == 0 and j == 14:
                        pe.wait_ge(sem("gate_lo"), GROUPS)
                    if n == 1 and j == 0:
                        pe.wait_ge(sem("z_read"), GROUPS)
                    if n >= 2 and j == 0:
                        pe.wait_ge(sem("resid_added"), n - 1)
                    piece(Pos(OUT0), 16 * n + j, acc[n % 2], NB, RB + 2 * j, j == 0, j == 15)
                    if n == 0 and j == 2:
                        turn_x_back(GROUPS - 1)
                    if n == 0 and j == 7:
                        scan(GROUPS - 1)
                    if n == 0 and j == 12:
                        pe.wait_ge(sem("cb_read"), GROUPS)
                        turn_gated(GROUPS - 1)
                    if n >= 1 and j == 2:
                        if n == 2:
                            pe.wait_ge(sem("y_read"), GROUPS)
                        if n == 3:
                            pe.wait_ge(sem("turned_lo"), 1)
                        turn_resid(n - 1, R_OUT + n, T_OUT + n)

            def mlp(base, R, T, U, T_carry):
                def up(c, u, fresh=False):
                    pos = Pos(base, c, PER_CHUNK)
                    off = 8 * u
                    for j in range(8):
                        if j == 0:
                            if u < 2:
                                pe.wait_ge(sem("resid_added"), c * 4 + (R - 1 + u))
                            else:
                                pe.wait_ge(sem("up_read"), c * 4 + (U + u - 1))
                            if fresh:
                                pe.wait_ge(sem("turned_lo"), T - 1)
                        if j == 6 and fresh:
                            pe.wait_ge(sem("turned_lo"), T)
                        piece(pos, off + j, acc[u % 2], NB, RA + 2 * j, j == 0, j == 7)
                        if j == 2 and fresh:
                            wait(pe, sem("turned_lo"), T - 2)
                            turn_resid(3, R, T)
                        if j == 2 and u > 0:
                            turn_up(c, u - 1)

                def turn_up(c, u):
                    pe.wait_ge(sem("up_read"), c * 4 + (U + u + 1))
                    pe.wait_ge(sem("turned_lo"), c * 4 + (T + u - 1))
                    transposes(to_channels(aux[u % 2]), lambda i, t: act[:, t, i * P:(i + 1) * P]).then_inc(sem("turned"), 1)

                def down(c, d, carry):
                    pos = Pos(base, c, PER_CHUNK)
                    for j in range(8):
                        if j == 0:
                            if d < 2:
                                pe.wait_ge(sem("up_read"), c * 4 + (U + 3 + d))
                            else:
                                pe.wait_ge(sem("resid_added"), c * 4 + (R + d - 1))
                            if d == 0:
                                pe.wait_ge(sem("turned_lo"), c * 4 + (T + 3))
                        if j == 6 and d == 0:
                            pe.wait_ge(sem("turned_lo"), c * 4 + (T + 4))
                        piece(pos, 32 + 8 * d + j, acc[d % 2], NB, RB + 2 * j, j == 0, j == 7)
                        if j == 2 and d == 0:
                            turn_up(c, 3)
                        if j == 2 and d > 0 and carry:
                            pe.wait_ge(sem("turned_lo"), T_carry + d - 2)
                            turn_resid(d - 1, c * 4 + (R + d), None)

                up(0, 0, True)
                with pe.Fori(0, 3) as c:
                    for u in range(1, 4):
                        up(c, u)
                    for d in range(4):
                        down(c, d, False)
                    up(c + 1, 0)
                for u in range(1, 4):
                    up(3, u)
                for d in range(4):
                    down(3, d, T_carry is not None)

            mlp(UP0, R_MLP0, T_MLP0, 0, T_MLP0_END)

            def turn_q(r):
                pe.wait_ge(sem("q_normed"), r + 1)
                pe.wait_ge(sem("kT_made"), r + 1)
                transposes(to_channels(aux[1]), lambda i, t: kq[:, t, i * P:(i + 1) * P]).then_inc(sem("q_turned"), 1)

            def scores_a(r):
                pe.wait_ge(sem("qT_made"), r + 1)
                for s in range(4):
                    pe.matmul(aux[1][:, 0, s * P:(s + 1) * P], qT[:, s, 0:P], kT[:, s, 0:P], start=True, stop=True)
                for s in range(2):
                    mm = pe.matmul(aux[1][:, 1, s * SEQ:(s + 1) * SEQ], qT[:, s, P:], kT[:, s, :], start=True, stop=True)
                mm.then_inc(sem("sa_ready"), 1)

            def scores_b(r):
                for s in range(2):
                    mm = pe.matmul(aux[0][:, 0, s * SEQ:(s + 1) * SEQ], qT[:, 2 + s, P:], kT[:, 2 + s, :], start=True, stop=True)
                mm.then_inc(sem("sb_ready"), 1)

            def turn_p(r):
                pe.wait_ge(sem("p_made"), r + 1)
                for k in range(2):
                    pe.transpose(aux[1][:, k, 0:P], s0[:, 2 * k, :], ident[:, :])
                    for i in range(2):
                        tr = pe.transpose(aux[1][:, k, (1 + i) * P:(2 + i) * P], s1[:, 2 * k, i * P:(i + 1) * P], ident[:, :])
                tr.then_inc(sem("p_turned"), 1)

            def apply_p(r):
                pe.wait_ge(sem("pt_made"), r + 1)
                for k in range(2):
                    v = [cols(vall[:, t, :], r * NB + k * 2 * HD, 2 * HD) for t in range(TT)]
                    o = slice(k * 2 * HD, (k + 1) * 2 * HD)
                    pe.matmul(aux[0][:, 0, o], pt[:, k, 0:P], v[0], start=True, stop=True)
                    pe.matmul(aux[0][:, 1, o], pt[:, k, P:2 * P], v[0], start=True, stop=False)
                    mm = pe.matmul(aux[0][:, 1, o], pt[:, k, 2 * P:], v[1], start=False, stop=True)
                mm.then_inc(sem("o_ready"), 1)

            def turn_o(r):
                pe.wait_ge(sem("o_normed"), r + 1)
                transposes(to_channels(aux[0]), lambda i, t: ob[:, t, i * P:(i + 1) * P]).then_inc(sem("o_turned"), 1)

            def pair(j, first):
                pos = Pos(ATT0, j, PER_PAIR)
                for i in range(PER_PAIR):
                    if first:
                        if i == 0:
                            pe.wait_ge(sem("turned_lo"), T_MLP0_END + 3)
                        if i == 6:
                            pe.wait_ge(sem("turned_lo"), T_MLP0_END + 4)
                        if i == 8:
                            pe.wait_ge(sem("resid_added"), R_WO - 1)
                        if i == 16:
                            pe.wait_ge(sem("resid_added"), R_WO)
                    else:
                        if i == 0:
                            wait(pe, sem("o_lo"), j - 1)
                        if i == 8:
                            pe.wait_ge(sem("k_read"), j)
                        if i == 16:
                            pe.wait_ge(sem("q_read"), j)
                    ps, region = ((aux[0], RA), (acc[0], RA), (acc[1], RC))[i // 8]
                    piece(pos, i, ps, NB, region + 2 * (i % 8), i % 8 == 0, i % 8 == 7)
                    if i == 2 and first:
                        turn_resid(3, R_WO, None)
                    if i == 22:
                        pe.wait_ge(sem("k_normed"), j + 1)
                        if not first:
                            pe.wait_ge(sem("pt_made"), j)
                        transposes(to_channels(aux[1]), lambda c, t: kq[:, t, c * P:(c + 1) * P]).then_inc(sem("k_turned"), 1)
                    if not first:
                        if i == 5:
                            turn_q(j - 1)
                        if i == 8:
                            scores_a(j - 1)
                        if i == 11:
                            pe.wait_ge(sem("v_read"), j + 1)
                            scores_b(j - 1)
                        if i == 16:
                            turn_p(j - 1)
                        if i == 18:
                            apply_p(j - 1)
                        if i == 21:
                            turn_o(j - 1)

            pair(0, True)
            with pe.Fori(1, 4) as j:
                pair(j, False)

            for i, (n, kt) in enumerate(WO_ORDER):
                if i == 0:
                    pe.wait_ge(sem("o_lo"), 3)
                    pe.wait_ge(sem("k_read"), 4)
                if i == 6:
                    pe.wait_ge(sem("q_read"), 4)
                if i == 12:
                    pe.wait_ge(sem("o_lo"), 4)
                if i == 16:
                    pe.wait_ge(sem("resid_added"), R_WO + 1)
                if i == 24:
                    pe.wait_ge(sem("resid_added"), R_WO + 2)
                piece(Pos(WO0), i, acc[n % 2], NB, RB + kt, kt == 0, kt == KT - 2)
                if i == 3:
                    turn_q(3)
                if i == 4:
                    scores_a(3)
                    scores_b(3)
                if i == 6:
                    turn_p(3)
                if i == 8:
                    apply_p(3)
                if i == 10:
                    turn_o(3)
                if i == 17:
                    turn_resid(0, R_WO + 1, None)
                if i == 19:
                    turn_resid(1, R_WO + 2, None)
                if i == 26:
                    pe.wait_ge(sem("turned_lo"), T_WO + 1)
                    turn_resid(2, R_WO + 3, None)

            mlp(UP1, R_MLP1, T_MLP1, 16, None)

        @block.scalar
        def _(act_e):
            a = act_e
            flat = lambda v: v.rearrange("(r c) -> r c", c=P)
            taps = ssm_conv_w[0].rearrange("j (r c) -> j r c", c=P)
            for r in range(2):
                for j in range(2):
                    a.dma_start(prow[j * CT:(j + 1) * CT, r, :], taps[2 * r + j]).then_inc(sem("rows_in"), 16)
            a.dma_start(prow[0:CT, 2, :], flat(ssm_conv_b[0])).then_inc(sem("rows_in"), 16)
            rows = [(ssm_norm_w[0], KT), (mlp_norm_w[0], KT), (mlp_norm_w[1], KT), (kv_norm_w, KT), (attn_norm_w[0], KT),
                    (ssm_out_norm_w[0], INNER // P), (k_norm_w, 1), (q_norm_w[0], 1), (subln_w[0], 2)]
            c = 0
            for v, n in rows:
                a.dma_start(prow[c:c + n, 3, :], flat(v)).then_inc(sem("rows_in"), 16)
                c += n
            a.dma_start(dtb, ssm_dt_bias.to_broadcast([P, HEADS])).then_inc(sem("dtb_in"), 16)
            a.dma_start(alog, ssm_a_log.to_broadcast([P, HEADS])).then_inc(sem("alog_in"), 16)
            a.dma_start(dskip[:, :], ssm_d.to_broadcast([P, HEADS])).then_inc(sem("dskip_in"), 16)
            for i, v in enumerate((lam_q1, lam_k1, lam_q2, lam_k2)):
                a.dma_start(lamv[:, i, :], v.to_broadcast([P, HD])).then_inc(sem("lam_in"), 16)

            def hi(pos, off):
                a.wait_ge(sem(f"raw_in{pos.slot(off)}"), pos.turn(off) * 32)
                wait(a, sem("w_used"), pos.done(off) - RING)
                s = pos.slot(off)
                a.activation(whi[:, s, :], raw[:, s, :], ACT.Copy).then_inc(sem("hi_made"), 1)

            a.wait_ge(sem("x_in"), 32)
            for t in range(TT):
                a.activation(xn[:, t, :], h[:, t, :], ACT.Square, accum_out=x_ss[:, t:t + 1]).then_inc(sem("x_squared"), 1)
            a.wait_ge(sem("alog_in"), 16)
            a.activation(alog, alog, ACT.Exp).then_inc(sem("a_made"), 1)
            a.wait_ge(sem("lam_summed"), 1)
            a.activation(lam_s, lam_s, ACT.Exp).then_inc(sem("lam_exp"), 1)
            a.wait_ge(sem("par_turned"), 1)
            a.activation(par[:, 0:C_NORM], acc[0][:, 0, 0:C_NORM], ACT.Copy, scale=0.5).then_inc(sem("par_made"), 1)
            a.activation(par[:, C_NORM:N_SUB], acc[0][:, 0, C_NORM:N_SUB], ACT.Copy).then_inc(sem("par_made"), 1)
            a.activation(par[:, N_SUB:], acc[0][:, 0, N_SUB:PARAMS], ACT.Copy, scale=1.0 - LAMBDA_INIT).then_inc(sem("par_made"), 1)
            hi(Pos(0), 0)
            a.wait_ge(sem("par_made"), 3)

            def split_hi(bank, kt, w):
                for i in range(4):
                    ins = a.activation(st[:, kt + i, 0, :] if isinstance(kt, int) else st[:, bass.ds(kt + i, 1), 0, :],
                                       turned_tile(bank, i), ACT.Copy, scale=param(w + i))
                return ins

            for i, bank in enumerate((aux[0], aux[1], acc[1], acc[0])):
                a.wait_ge(sem("x_turned"), i + 1)
                split_hi(bank, RA + 4 * i, N_SSM + 4 * i).then_inc(sem("x_hi"), 1)

            def tail(j, r, end):
                if j == 1:
                    a.wait_ge(sem("x_conv_lin"), r * 4 + 4)
                    a.wait_ge(sem("x_conv"), r * 2 + 1)
                    a.activation(th, cvx[:, 2:4, :], ACT.Tanh).then_inc(sem("x_tanh"), 1)
                if j == 2:
                    a.wait_ge(sem("w_used"), Pos(IN0, r, PER_GROUP).done(19))
                    wait(a, sem("gated"), r)
                    a.activation(zg, acc[1][:, :, :], ACT.Tanh, scale=0.5).then_inc(sem("z_tanh"), 1)
                if j == 12:
                    a.wait_ge(sem("gated"), r + 1)
                    for t in range(TT):
                        ins = a.activation(xraw[:, t, :], gbuf[:, t, :], ACT.Square, accum_out=g_ss[:, t:t + 1])
                    ins.then_inc(sem("g_squared"), 1)
                if j == 14:
                    a.wait_ge(sem("g_rstd"), r + 1)
                    for t in range(TT):
                        ins = a.activation(gbuf[:, t, :], gbuf[:, t, :], ACT.Copy, scale=g_rs[:, t:t + 1])
                    ins.then_inc(sem("g_normed"), 1)
                if j == end:
                    a.wait_ge(sem("g_turned"), r + 1)
                    split_hi(aux[0], r * 4 + RB, r * 4 + N_OUT).then_inc(sem("gate_hi"), 1)

            def group(g, first):
                pos = Pos(IN0, g, PER_GROUP)
                for j in range(PER_GROUP):
                    hi(pos, j)
                    if j == 1 and first:
                        a.wait_ge(sem("dt_abs"), 1)
                        a.activation(dts[:, 2, :], dts[:, 1, :], ACT.Exp, scale=-1.0).then_inc(sem("dt_exp"), 1)
                    if j == 6 and first:
                        a.wait_ge(sem("decays_ready"), 1)
                        a.activation(rowsb[0:HEADS, :], aux[1][0:HEADS, 0, 0:SEQ], ACT.Copy).then_inc(sem("rows_made"), 1)
                        a.activation(colv[:, :, :].rearrange("p n h -> p (n h)"), aux[1][:, 1, 0:6 * HEADS], ACT.Copy).then_inc(sem("decays_read"), 1)
                    if j == 6:
                        a.wait_ge(sem("w_used"), pos.done(3))
                        a.activation(bcraw, aux[0][:, :, 0:2 * P], ACT.Copy).then_inc(sem("bc_read"), 1)
                    if j == 8:
                        a.wait_ge(sem("bc_turned"), g + 1)
                        for i in range(2):
                            ct = g + (INNER // P + i * GROUPS)
                            ins = a.activation(bct[:, i, :], aux[0][:, 0, i * SEQ:(i + 1) * SEQ], ACT.Identity,
                                               bias=conv_b(ct), scale=conv_w(3, ct))
                        ins.then_inc(sem("bc_tap"), 1)
                    if j == 9:
                        a.wait_ge(sem("bc_conv_lin"), g + 1)
                        if not first:
                            a.wait_ge(sem("x_conv"), g * 2)
                        a.activation(th, bct, ACT.Tanh).then_inc(sem("bc_tanh"), 1)
                    if not first:
                        tail(j, g - 1, 18)
                    if j == 14:
                        a.wait_ge(sem("cb_ready"), g + 1)
                        if not first:
                            a.wait_ge(sem("m_made"), g)
                        a.activation(cb, aux[0][:, 1, 0:3 * P], ACT.Copy).then_inc(sem("cb_read"), 1)
                        a.wait_ge(sem("w_used"), pos.done(11))
                        if not first:
                            a.wait_ge(sem("g_squared"), g)
                        a.activation(xraw, acc[0][:, :, :], ACT.Copy).then_inc(sem("x_read"), 1)
                    if j == 15:
                        a.wait_ge(sem("masked"), g * 2 + 1)
                        a.activation(m1, m1, ACT.Exp).then_inc(sem("decay_made"), 1)
                    if j == 16:
                        a.wait_ge(sem("masked"), g * 2 + 2)
                        a.activation(m0, m0, ACT.Exp).then_inc(sem("decay_made"), 1)
                    if j == 17:
                        a.wait_ge(sem("x_raw_turned"), g + 1)
                        for i in range(4):
                            ct = g * 4 + i
                            a.activation(cvx[:, i, :], turned_tile(aux[1], i), ACT.Identity,
                                         bias=conv_b(ct), scale=conv_w(3, ct)).then_inc(sem("x_tap"), 1)
                    if j == 19:
                        a.wait_ge(sem("x_conv_lin"), g * 4 + 2)
                        a.wait_ge(sem("bc_conv"), g + 1)
                        a.activation(th, cvx[:, 0:2, :], ACT.Tanh).then_inc(sem("x_tanh"), 1)

            group(0, True)
            with a.Fori(1, GROUPS) as g:
                group(g, False)

            squared = [0]

            def resid_squares(n, added):
                a.wait_ge(sem("resid_added"), added)
                wait(a, sem("h_squared"), squared[0])
                squared[0] += 1
                for t in range(TT):
                    ins = a.activation(act[:, t, :], h[:, t, n * NB:(n + 1) * NB], ACT.Square, accum_out=h_ss[:, t * 4 + n:t * 4 + n + 1])
                ins.then_inc(sem("h_squared"), 1)

            def resid_hi(n, turned, targets):
                a.wait_ge(sem("turned"), turned)
                for region, w in targets:
                    ins = split_hi(aux[n % 2], region + 4 * n, w + 4 * n)
                ins.then_inc(sem("turned_hi"), 1)

            to_mlp0, to_att, to_mlp1 = [(RA, N_MLP0)], [(RA, N_KV), (RC, N_ATT)], [(RA, N_MLP1)]

            for n in range(4):
                for j in range(16):
                    hi(Pos(OUT0), 16 * n + j)
                    if n == 0:
                        tail(j, GROUPS - 1, 15)
                    if n >= 1 and j == 3:
                        resid_squares(n - 1, R_OUT + n)
                    if n >= 1 and j == 5:
                        resid_hi(n - 1, T_OUT + n, to_mlp0)

            def mlp(base, R, T, U, T_carry, before, after):
                def relu(c, u):
                    a.wait_ge(sem("w_used"), Pos(base, c, PER_CHUNK).done(8 * u + 7))
                    if u > 0:
                        a.wait_ge(sem("turned"), c * 4 + (T + u))
                    else:
                        a.wait_ge(sem("turned"), c * 4 + T)
                        a.wait_ge(sem("h_squared"), squared[0])
                    a.activation(act, acc[u % 2][:, :, :], ACT.Relu).then_inc(sem("relu_made"), 1)

                def up_hi(c, u):
                    a.wait_ge(sem("turned"), c * 4 + (T + u + 1))
                    a.activation(st[:, RB + 4 * u:RB + 4 * u + 4, 0, :], whole(aux[u % 2]), ACT.Copy).then_inc(sem("turned_hi"), 1)

                def run(c, off, steps):
                    for j in range(8):
                        hi(Pos(base, c, PER_CHUNK), off + j)
                        steps(j)

                def after_up(c, u):
                    def steps(j):
                        if j == 2:
                            relu(c, u)
                        if j == 5:
                            up_hi(c, u)
                    return steps

                def after_resid(n, added, turned, targets):
                    def steps(j):
                        if j == 3 and targets:
                            resid_squares(n, added)
                        if j == 5 and targets:
                            resid_hi(n, turned, targets)
                    return steps

                run(0, 0, after_resid(3, R, T, before))
                with a.Fori(0, 3) as c:
                    for u in range(1, 5):
                        run(c, 8 * u, after_up(c, u - 1))
                    for d in range(1, 5):
                        run(c, 32 + 8 * d, after_resid(d - 1, None, None, None))
                for u in range(1, 5):
                    run(3, 8 * u, after_up(3, u - 1))
                for d in range(1, 4):
                    run(3, 32 + 8 * d, after_resid(d - 1, R + 12 + d, (T_carry or 0) + d, after))

            mlp(UP0, R_MLP0, T_MLP0, 0, T_MLP0_END, to_mlp0, to_att)

            def read_scaled(dst, ps):
                for t in range(TT):
                    ins = a.activation(dst(t), ps[:, t, :], ACT.Copy, scale=h_rs[:, t:t + 1])
                return ins

            def read_q(r):
                a.wait_ge(sem("w_used"), Pos(ATT0, r, PER_PAIR).done(23))
                a.wait_ge(sem("k_turned"), r + 1)
                read_scaled(lambda t: kq[:, t, :], acc[1]).then_inc(sem("q_read"), 1)

            def make_kT(r):
                a.wait_ge(sem("k_turned"), r + 1)
                a.activation(kT, whole(aux[1]), ACT.Copy, scale=param(N_K)).then_inc(sem("kT_made"), 1)

            def make_qT(r):
                a.wait_ge(sem("q_turned"), r + 1)
                a.activation(qT, whole(aux[1]), ACT.Copy, scale=param(N_Q)).then_inc(sem("qT_made"), 1)

            def exps(r, t):
                a.wait_ge(sem("max_made"), r * 2 + (t + 1))
                for s in range(4):
                    v = (s0, s1)[t][:, s, :]
                    n = t * 4 + s
                    ins = a.activation(v, v, ACT.Exp, bias=kq_ss[:, n:n + 1], scale=HD ** -0.5, accum_out=kq_rs[:, n:n + 1])
                ins.then_inc(sem("exp_made"), 1)

            def make_pt(r):
                a.wait_ge(sem("p_turned"), r + 1)
                a.activation(pt, aux[1][:, :, 0:3 * P], ACT.Copy).then_inc(sem("pt_made"), 1)

            def o_squares(r):
                a.wait_ge(sem("o_ready"), r + 1)
                for t in range(TT):
                    for k in range(2):
                        o = slice(k * 2 * HD, (k + 1) * 2 * HD)
                        n = t * 2 + k
                        ins = a.activation(ob[:, t, o], aux[0][:, t, o], ACT.Square, accum_out=o_ss[:, n:n + 1])
                ins.then_inc(sem("o_squared"), 1)

            def o_norm(r):
                a.wait_ge(sem("o_rstd"), r + 1)
                for t in range(TT):
                    for k in range(2):
                        o = slice(k * 2 * HD, (k + 1) * 2 * HD)
                        n = t * 2 + k
                        ins = a.activation(ob[:, t, o], aux[0][:, t, o], ACT.Copy, scale=o_rs[:, n:n + 1])
                ins.then_inc(sem("o_normed"), 1)

            def o_hi(r):
                a.wait_ge(sem("o_turned"), r + 1)
                for i in range(4):
                    ins = a.activation(one_tile(st, r * 4 + (RB + i), 0), turned_tile(aux[0], i), ACT.Copy, scale=param(N_SUB + i % 2))
                ins.then_inc(sem("o_hi"), 1)

            def pair(j, first):
                pos = Pos(ATT0, j, PER_PAIR)
                for i in range(PER_PAIR):
                    hi(pos, i)
                    if first and i == 3:
                        resid_squares(3, R_WO)
                    if first and i == 5:
                        resid_hi(3, T_MLP0_END + 4, to_att)
                    if i == 10:
                        if first:
                            a.wait_ge(sem("h_rstd"), 1)
                        a.wait_ge(sem("w_used"), pos.done(7))
                        read_scaled(lambda t: cols(vall[:, t, :], j * NB, NB), aux[0]).then_inc(sem("v_read"), 1)
                    if i == 18:
                        a.wait_ge(sem("w_used"), pos.done(15))
                        if not first:
                            a.wait_ge(sem("q_turned"), j)
                        read_scaled(lambda t: kq[:, t, :], acc[0]).then_inc(sem("k_read"), 1)
                    if not first:
                        r = j - 1
                        if i == 1:
                            make_kT(r)
                        if i == 2:
                            read_q(r)
                        if i == 7:
                            make_qT(r)
                        if i == 14:
                            exps(r, 0)
                        if i == 15:
                            exps(r, 1)
                        if i == 17:
                            make_pt(r)
                        if i == 19:
                            o_squares(r)
                        if i == 21:
                            o_norm(r)
                        if i == 23:
                            o_hi(r)

            pair(0, True)
            with a.Fori(1, 4) as j:
                pair(j, False)

            for i in range(len(WO_ORDER)):
                hi(Pos(WO0), i)
                if i == 1:
                    make_kT(3)
                if i == 2:
                    read_q(3)
                if i == 5:
                    make_qT(3)
                if i == 7:
                    exps(3, 0)
                    exps(3, 1)
                if i == 8:
                    make_pt(3)
                if i == 10:
                    o_squares(3)
                    o_norm(3)
                if i == 12:
                    o_hi(3)
                for n, at_sq, at_hi in ((0, 17, 20), (1, 19, 22), (2, 27, 29)):
                    if i == at_sq:
                        resid_squares(n, R_WO + n + 1)
                    if i == at_hi:
                        resid_hi(n, T_WO + n + 1, to_mlp1)

            mlp(UP1, R_MLP1, T_MLP1, 16, None, to_mlp1, None)

        @block.vector
        def _(v):
            link = Chain(v, sem("v_chain"))

            def lo(pos, off):
                v.wait_ge(sem("hi_made"), pos.done(off))
                s = pos.slot(off)
                v.tensor_tensor(wlo[:, s, :], raw[:, s, :], whi[:, s, :].bitcast(F32), ALU.subtract).then_inc(sem("lo_made"), 1)

            def split_lo(bank, kt, w):
                for i in range(4):
                    ins = v.scalar_tensor_tensor(one_tile(st, kt + i, 1), turned_tile(bank, i), param(w + i),
                                                 one_tile(st, kt + i, 0).bitcast(F32), ALU.mult, ALU.subtract)
                return ins

            def mean_eps(out, sums, n, eps):
                return v.tensor_scalar(out, sums, 1.0 / n, eps, ALU.mult, ALU.add)

            v.wait_ge(sem("lam_in"), 4 * 16)
            for i in range(2):
                last = v.tensor_tensor(lamt[:, i, :], lamv[:, 2 * i, :], lamv[:, 2 * i + 1, :], ALU.mult)
            link(last)
            v.tensor_reduce(lam_s, lamt, AX.X, ALU.add).then_inc(sem("lam_summed"), 1)
            link(v.memset(coef, 1.0))
            v.wait_ge(sem("x_squared"), TT)
            mean_eps(x_ss, x_ss, D, EPS).then_inc(sem("x_ms"), 1)
            v.wait_ge(sem("x_rstd"), 1)
            for t in range(TT):
                v.tensor_scalar(xn[:, t, :], h[:, t, :], x_rs[:, t:t + 1], None, ALU.mult).then_inc(sem("xn_made"), 1)
            v.wait_ge(sem("lam_exp"), 1)
            minus_lam = coef.rearrange("p (a b) -> p a b", b=2)[:, :, 1]
            link(v.scalar_tensor_tensor(lam_s[:, 0:1], lam_s[:, 1:2], LAMBDA_INIT, lam_s[:, 0:1], ALU.subtract, ALU.subtract))
            link(v.tensor_copy(minus_lam, lam_s[:, 0:1].to_broadcast([P, 4])))
            v.wait_ge(sem("par_made"), 3)
            lo(Pos(0), 0)
            for i, bank in enumerate((aux[0], aux[1], acc[1], acc[0])):
                v.wait_ge(sem("x_hi"), i + 1)
                split_lo(bank, RA + 4 * i, N_SSM + 4 * i).then_inc(sem("x_split"), 1)

            def softplus_dt_a():
                tm = lambda i: dts[:, i, :]
                tv = lambda i: dts[:, i, :].rearrange("p (t h) -> p t h", t=TT)
                v.wait_ge(sem("w_used"), 1)
                v.wait_ge(sem("dtb_in"), 16)
                v.tensor_tensor(tv(0), aux[0][:, :, 0:HEADS], dtb.unsqueeze(1).to_broadcast([P, TT, HEADS]), ALU.add).then_inc(sem("dt_read"), 1)
                v.wait_ge(sem("dt_read"), 1)
                v.scalar_tensor_tensor(tm(1), tm(0), -1.0, tm(0), ALU.mult, ALU.max).then_inc(sem("dt_abs"), 1)
                v.wait_ge(sem("dt_exp"), 1)
                link(v.tensor_scalar(tm(3), tm(2), 2.0, None, ALU.add))
                link(v.reciprocal(tm(4), tm(3)))
                link(v.tensor_tensor(tm(5), tm(2), tm(4), ALU.mult))
                link(v.tensor_tensor(tm(6), tm(5), tm(5), ALU.mult))
                link(v.tensor_scalar(tm(7), tm(6), 1.0 / 17, None, ALU.mult))
                for n in (15, 13, 11, 9, 7, 5, 3):
                    link(v.scalar_tensor_tensor(tm(7), tm(7), 1.0 / n, tm(6), ALU.add, ALU.mult))
                link(v.scalar_tensor_tensor(tm(7), tm(7), 1.0, tm(5), ALU.add, ALU.mult))
                link(v.tensor_scalar(tm(1), tm(0), 0.0, None, ALU.max))
                link(v.scalar_tensor_tensor(dt[:, :, :].rearrange("p t h -> p (t h)"), tm(7), 2.0, tm(1), ALU.mult, ALU.add))
                v.wait_ge(sem("a_made"), 1)
                v.scalar_tensor_tensor(da, dt[:, :, :], -1.0, alog.unsqueeze(1).to_broadcast([P, TT, HEADS]),
                                       ALU.mult, ALU.mult).then_inc(sem("da_made"), 1)

            def conv(dst, src, ct):
                for sh in range(1, TAPS):
                    ins = v.scalar_tensor_tensor(dst[:, sh:], src[:, 0:SEQ - sh], conv_w(TAPS - 1 - sh, ct), dst[:, sh:], ALU.mult, ALU.add)
                    if sh < TAPS - 1:
                        link(ins)
                return ins

            def by_head(table, r):
                return cols(table, r * HG, HG).unsqueeze(2).to_broadcast([P, HG, HP])

            heads = lambda ap: ap.rearrange("p (h c) -> p h c", h=HG)

            def tail(j, r, end):
                if j == 0:
                    v.wait_ge(sem("x_tap"), r * 4 + 4)
                    conv(cvx[:, 3, :], turned_tile(aux[1], 3), r * 4 + 3).then_inc(sem("x_conv_lin"), 1)
                    v.wait_ge(sem("x_tanh"), r * 2 + 1)
                    v.scalar_tensor_tensor(cvx[:, 0:2, :], th, 1.0, cvx[:, 0:2, :], ALU.add, ALU.mult).then_inc(sem("x_conv"), 1)
                if j == 1:
                    v.wait_ge(sem("decay_made"), r * 2 + 2)
                    v.wait_ge(sem("cb_read"), r + 1)
                    v.tensor_tensor(m1, m1, cb[:, SEQ:].unsqueeze(1).to_broadcast([P, HG, P]), ALU.mult)
                    v.tensor_tensor(m0[:, 0:4, :], m0[:, 0:4, :], cb[:, 0:SEQ].unsqueeze(1).to_broadcast([P, 4, SEQ]), ALU.mult)
                if j == 2:
                    v.wait_ge(sem("x_tanh"), r * 2 + 2)
                    v.scalar_tensor_tensor(cvx[:, 2:4, :], th, 1.0, cvx[:, 2:4, :], ALU.add, ALU.mult).then_inc(sem("x_conv"), 1)
                    v.tensor_tensor(m0[:, 4:8, :], m0[:, 4:8, :], cb[:, 0:SEQ].unsqueeze(1).to_broadcast([P, 4, SEQ]), ALU.mult).then_inc(sem("m_made"), 1)
                if j == 3:
                    v.wait_ge(sem("z_tanh"), r + 1)
                    v.scalar_tensor_tensor(zg, zg, 1.0, acc[1][:, :, :], ALU.add, ALU.mult).then_inc(sem("z_read"), 1)
                if j == 5:
                    v.wait_ge(sem("x_back"), r + 1)
                    for t in range(TT):
                        v.tensor_tensor(heads(xdt[:, t, :]), heads(aux[1][:, t, :]), by_head(dt[:, t, :], r), ALU.mult)
                if j == 6:
                    v.wait_ge(sem("dskip_in"), 16)
                    for t in range(TT):
                        ins = v.tensor_tensor(heads(gbuf[:, t, :]), heads(aux[1][:, t, :]), by_head(dskip[:, :], r), ALU.mult)
                    ins.then_inc(sem("xdt_made"), 1)
                if j == 11:
                    v.wait_ge(sem("y_ready"), r + 1)
                    v.tensor_tensor(gbuf, aux[1][:, :, :], gbuf, ALU.add).then_inc(sem("y_read"), 1)
                if j == 12:
                    v.wait_ge(sem("y_read"), r + 1)
                    v.tensor_tensor(gbuf, gbuf, zg, ALU.mult).then_inc(sem("gated"), 1)
                if j == 13:
                    v.wait_ge(sem("g_squared"), r + 1)
                    mean_eps(g_ms, g_ss, GC, 4 * EPS).then_inc(sem("g_ms"), 1)
                if j == end:
                    v.wait_ge(sem("gate_hi"), r + 1)
                    split_lo(aux[0], r * 4 + RB, r * 4 + N_OUT).then_inc(sem("gate_lo"), 1)

            def group(g, first):
                pos = Pos(IN0, g, PER_GROUP)
                for j in range(PER_GROUP):
                    lo(pos, j)
                    if not first:
                        tail(j, g - 1, 18)
                    if j == 9:
                        v.wait_ge(sem("bc_tap"), g + 1)
                        for i in range(2):
                            ins = conv(bct[:, i, :], aux[0][:, 0, i * SEQ:(i + 1) * SEQ], g + (INNER // P + i * GROUPS))
                        ins.then_inc(sem("bc_conv_lin"), 1)
                    if j == 10:
                        v.wait_ge(sem("bc_tanh"), g + 1)
                        v.scalar_tensor_tensor(bct, th, 1.0, bct, ALU.add, ALU.mult).then_inc(sem("bc_conv"), 1)
                    if j == 12:
                        v.wait_ge(sem("row_in"), g * 16 + 16)
                        if first:
                            v.wait_ge(sem("decays_read"), 1)
                        colp = lambda n0, n: cols3(colv, n0, n, g * HG).rearrange("p c h -> p h c").unsqueeze(3).to_broadcast([P, HG, n, CH])
                        lch = lambda ap, n: ap.rearrange("p h (c l) -> p h c l", c=n)
                        v.tensor_tensor(lch(m1, 2), lch(m0[:, :, P:], 2), colp(4, 2), ALU.add).then_inc(sem("exponents"), 1)
                    if j == 13:
                        v.wait_ge(sem("exponents"), g * 2 + 1)
                        v.tensor_tensor(lch(m0, 4), lch(m0, 4), colp(0, 4), ALU.add).then_inc(sem("exponents"), 1)
                    if j in (17, 18, 19):
                        i = j - 17
                        v.wait_ge(sem("x_tap"), g * 4 + (2 if i < 2 else 4))
                        conv(cvx[:, i, :], turned_tile(aux[1], i), g * 4 + i).then_inc(sem("x_conv_lin"), 1)
                    if first and j == 0:
                        softplus_dt_a()

            group(0, True)
            GROUP_LINKS = 12
            with v.Fori(1, GROUPS) as g:
                link.enter(g, 1, GROUP_LINKS)
                group(g, False)
                link.leave(GROUPS - 1)

            def add_resid(n, pos, last, scaled):
                v.wait_ge(sem("w_used"), pos.done(last))
                hb = h[:, :, n * NB:(n + 1) * NB]
                ps = acc[n % 2]
                if not scaled:
                    v.tensor_tensor(hb, ps[:, :, :], hb, ALU.add).then_inc(sem("resid_added"), 1)
                    return
                for t in range(TT):
                    ins = v.scalar_tensor_tensor(hb[:, t], ps[:, t, :], h_rs[:, t:t + 1], hb[:, t], ALU.mult, ALU.add)
                ins.then_inc(sem("resid_added"), 1)

            def resid_lo(n, turned, targets):
                v.wait_ge(sem("turned_hi"), turned)
                for region, w in targets:
                    ins = split_lo(aux[n % 2], region + 4 * n, w + 4 * n)
                ins.then_inc(sem("turned_lo"), 1)

            def resid_ms(squared):
                v.wait_ge(sem("h_squared"), squared)
                link(v.tensor_reduce(h_ms, h_ss.rearrange("p (t n) -> p t n", t=TT), AX.X, ALU.add))
                return mean_eps(h_ms, h_ms, D, EPS)

            to_mlp0, to_att, to_mlp1 = [(RA, N_MLP0)], [(RA, N_KV), (RC, N_ATT)], [(RA, N_MLP1)]

            for n in range(4):
                for j in range(16):
                    lo(Pos(OUT0), 16 * n + j)
                    if n == 0:
                        tail(j, GROUPS - 1, 15)
                    if n >= 1 and j == 2:
                        add_resid(n - 1, Pos(OUT0), 16 * n - 1, False)
                    if n >= 1 and j == 5:
                        resid_lo(n - 1, T_OUT + n, to_mlp0)

            def mlp(base, R, T, U, T_carry, before, after, prev, squared):
                def square(c, u):
                    v.wait_ge(sem("relu_made"), c * 4 + (U + u + 1))
                    v.scalar_tensor_tensor(act, acc[u % 2][:, :, :], 0.0, act, ALU.max, ALU.mult).then_inc(sem("up_read"), 1)

                def up_lo(c, u):
                    v.wait_ge(sem("turned_hi"), c * 4 + (T + u + 1))
                    v.tensor_tensor(st[:, RB + 4 * u:RB + 4 * u + 4, 1, :], whole(aux[u % 2]),
                                    st[:, RB + 4 * u:RB + 4 * u + 4, 0, :].bitcast(F32), ALU.subtract).then_inc(sem("turned_lo"), 1)

                def run(c, off, steps):
                    for j in range(8):
                        lo(Pos(base, c, PER_CHUNK), off + j)
                        steps(j)

                def after_up(c, u):
                    def steps(j):
                        if j == 2:
                            square(c, u)
                        if j == 5:
                            up_lo(c, u)
                    return steps

                def after_down(c, d, carry):
                    def steps(j):
                        if j == 2:
                            add_resid(d, Pos(base, c, PER_CHUNK), 32 + 8 * d + 7, True)
                        if j == 5 and carry:
                            resid_lo(d, T_carry + d + 1, after)
                    return steps

                def start(j):
                    if j == 2:
                        prev()
                    if j == 5:
                        resid_lo(3, T, before)
                    if j == 6:
                        link(resid_ms(squared))
                        link(v.reciprocal(h_rs, h_ms))

                run(0, 0, start)
                with v.Fori(0, 3) as c:
                    for u in range(1, 5):
                        run(c, 8 * u, after_up(c, u - 1))
                    for d in range(1, 5):
                        run(c, 32 + 8 * d, after_down(c, d - 1, False))
                for u in range(1, 5):
                    run(3, 8 * u, after_up(3, u - 1))
                for d in range(1, 4):
                    run(3, 32 + 8 * d, after_down(3, d - 1, after is not None))

            mlp(UP0, R_MLP0, T_MLP0, 0, T_MLP0_END, to_mlp0, to_att,
                lambda: add_resid(3, Pos(OUT0), 63, False), 4)

            def norm_sums(r, read):
                v.wait_ge(sem(read), r + 1)
                segs = lambda ap: ap.rearrange("p t (s c) -> p (t s) c", c=HD)
                link(v.tensor_tensor(act, kq, kq, ALU.mult))
                link(v.tensor_reduce(kq_ss, segs(act), AX.X, ALU.add))
                mean_eps(kq_ss, kq_ss, HD, EPS).then_inc(sem("kq_ms"), 1)

            def normalise(count, signal):
                v.wait_ge(sem("kq_rstd"), count)
                kqs = kq.rearrange("p t (s c) -> p (t s) c", c=HD)
                v.tensor_tensor(kqs, kqs, kq_rs.unsqueeze(2).to_broadcast([P, 8, HD]), ALU.mult).then_inc(sem(signal), 1)

            def maxima(r, t):
                if t == 0:
                    v.wait_ge(sem("sa_ready"), r + 1)
                    link(v.tensor_tensor(s0, aux[1][:, 0, :].rearrange("p (s k) -> p s k", s=4), mask0.unsqueeze(1).to_broadcast([P, 4, P]), ALU.add))
                    link(v.tensor_reduce(kq_ss[:, 0:4], s0, AX.X, ALU.max))
                else:
                    m = mask1.unsqueeze(1).to_broadcast([P, 2, SEQ])
                    v.tensor_tensor(s1[:, 0:2, :], aux[1][:, 1, :].rearrange("p (s k) -> p s k", s=2), m, ALU.add)
                    v.wait_ge(sem("sb_ready"), r + 1)
                    link(v.tensor_tensor(s1[:, 2:4, :], aux[0][:, 0, :].rearrange("p (s k) -> p s k", s=2), m, ALU.add))
                    link(v.tensor_reduce(kq_ss[:, 4:8], s1, AX.X, ALU.max))
                c = kq_ss[:, 4 * t:4 * t + 4]
                v.tensor_scalar(c, c, -(HD ** -0.5), None, ALU.mult).then_inc(sem("max_made"), 1)

            def combine(r):
                v.wait_ge(sem("exp_made"), 2 * (r + 1))
                link(v.reciprocal(kq_rs, kq_rs))
                link(v.tensor_tensor(kq_rs, kq_rs, coef, ALU.mult))
                for k in range(2):
                    for t, sc in enumerate((s0, s1)):
                        n = t * 4 + 2 * k
                        link(v.tensor_scalar(sc[:, 2 * k + 1, :], sc[:, 2 * k + 1, :], kq_rs[:, n + 1:n + 2], None, ALU.mult))
                        ins = v.scalar_tensor_tensor(sc[:, 2 * k, :], sc[:, 2 * k, :], kq_rs[:, n:n + 1], sc[:, 2 * k + 1, :], ALU.mult, ALU.add)
                ins.then_inc(sem("p_made"), 1)

            def o_means(r):
                v.wait_ge(sem("o_squared"), r + 1)
                mean_eps(o_ss, o_ss, 2 * HD, EPS).then_inc(sem("o_ms"), 1)

            def o_lo(r):
                v.wait_ge(sem("o_hi"), r + 1)
                for i in range(4):
                    kt = r * 4 + (RB + i)
                    ins = v.scalar_tensor_tensor(one_tile(st, kt, 1), turned_tile(aux[0], i), param(N_SUB + i % 2),
                                                 one_tile(st, kt, 0).bitcast(F32), ALU.mult, ALU.subtract)
                ins.then_inc(sem("o_lo"), 1)

            def pair(j, first):
                pos = Pos(ATT0, j, PER_PAIR)
                for i in range(PER_PAIR):
                    lo(pos, i)
                    if first and i == 2:
                        add_resid(3, Pos(UP0, 3, PER_CHUNK), PER_CHUNK - 1, True)
                    if first and i == 5:
                        resid_lo(3, T_MLP0_END + 4, to_att)
                    if first and i == 6:
                        resid_ms(8).then_inc(sem("h_ms"), 1)
                    if i == 19:
                        if not first:
                            v.wait_ge(sem("o_ready"), j)
                        norm_sums(j, "k_read")
                    if i == 20:
                        normalise(j * 2 + 1, "k_normed")
                    if not first:
                        r = j - 1
                        if i == 3:
                            norm_sums(r, "q_read")
                        if i == 4:
                            normalise(r * 2 + 2, "q_normed")
                        if i == 12:
                            maxima(r, 0)
                        if i == 13:
                            maxima(r, 1)
                        if i == 16:
                            combine(r)
                        if i == 20:
                            o_means(r)
                        if i == 23:
                            o_lo(r)

            pair(0, True)
            PAIR_LINKS = 14
            with v.Fori(1, 4) as j:
                link.enter(j, 1, PAIR_LINKS)
                pair(j, False)
                link.leave(3)

            for i in range(len(WO_ORDER)):
                lo(Pos(WO0), i)
                if i == 2:
                    norm_sums(3, "q_read")
                if i == 3:
                    normalise(8, "q_normed")
                if i == 6:
                    maxima(3, 0)
                    maxima(3, 1)
                if i == 8:
                    combine(3)
                if i == 10:
                    o_means(3)
                if i == 12:
                    o_lo(3)
                for n, last, at_add, at_lo in ((0, 13, 16, 20), (1, 15, 18, 22), (2, 23, 26, 29)):
                    if i == at_add:
                        add_resid(n, Pos(WO0), last, False)
                    if i == at_lo:
                        resid_lo(n, T_WO + n + 1, to_mlp1)

            mlp(UP1, R_MLP1, T_MLP1, 16, None, to_mlp1, None,
                lambda: add_resid(3, Pos(WO0), 31, False), 12)
            add_resid(3, Pos(UP1, 3, PER_CHUNK), PER_CHUNK - 1, True)

        @block.gpsimd
        def _(gp):
            link = Chain(gp, sem("gp_chain"))

            def keep(ap, pattern, base, mult, fill, then=None, op=ALU.is_ge):
                ins = gp.affine_select(out=ap, in_=ap, compare_op=op, fill=fill, base=base, pattern=pattern, channel_multiplier=mult)
                if then:
                    ins.then_inc(sem(then), 1)
                else:
                    link(ins)

            def rsqrt(out, in_, signal):
                gp.tensor_tensor(out, in_, nhalf[:, 0:out.shape[1]], ALU.pow).then_inc(sem(signal), 1)

            link(gp.memset(nhalf, -0.5))
            gp.memset(ident[:, :], 0.0).then_inc(sem("ident_made"), 1)
            gp.wait_ge(sem("ident_made"), 1)
            keep(ident[:, :], [[-1, P]], 0, 1, 1.0, "ident_made", ALU.not_equal)
            gp.wait_ge(sem("x_ms"), 1)
            rsqrt(x_rs, x_ss, "x_rstd")
            km = lambda i: kmat[:, i, :]
            gp.memset(kmat[:, 2:5, :], 1.0)
            gp.memset(kmat[:, 1, 0:CH], 1.0)
            gp.memset(kmat[:, 1, CH:], -1.0)
            gp.memset(kmat[:, 0, 0:CH], -1.0)
            link(gp.memset(kmat[:, 0, CH:], 0.0))
            keep(kmat[:, 0, 0:CH], [[1, CH]], 0, -1, 0.0)
            keep(kmat[:, 1, 0:CH], [[-1, CH]], -1, 1, 0.0)
            keep(kmat[:, 1, 0:CH], [[0, CH]], CH - 1, -1, 0.0)
            keep(kmat[:, 1, CH:], [[1, CH]], CH, -1, 0.0)
            keep(kmat[:, 1, CH:], [[0, CH]], -CH, 1, 0.0)
            keep(km(2), [[-1, P]], -1, 1, 0.0)
            keep(km(3), [[0, P]], CH - 1, -1, 0.0)
            keep(kmat[:, 4, CH:], [[0, CH]], -CH, 1, 0.0)
            keep(km(4), [[1, P]], 0, -1, 0.0, "kmat_made")
            link(gp.memset(no_later[:, :], 0.0))
            keep(no_later[:, :], [[1, P]], 0, -1, NEG)
            gp.wait_ge(sem("rows_made"), 1)
            gp.dma_start(rows_dram, rowsb[0:HEADS, :]).then_inc(sem("rows_out"), 16)
            gp.wait_ge(sem("rows_out"), 16)

            def rows_of(g):
                src = rows_dram[one(g * HG, HG), :]
                gp.dma_start(m0, src.unsqueeze(0).to_broadcast([P, HG, SEQ])).then_inc(sem("row_in"), 16)

            def gate_rstd(r):
                gp.wait_ge(sem("g_ms"), r + 1)
                rsqrt(g_rs, g_ms, "g_rstd")

            def masks(g):
                later = no_later[:, :].unsqueeze(1).to_broadcast([P, HG, P])
                for i, m in enumerate((m1, m0[:, :, 0:P])):
                    gp.wait_ge(sem("exponents"), g * 2 + (i + 1))
                    gp.tensor_tensor(m, m, later, ALU.add).then_inc(sem("masked"), 1)

            gp.wait_ge(sem("decays_read"), 1)
            rows_of(0)
            masks(0)
            with gp.Fori(1, GROUPS) as g:
                gp.wait_ge(sem("y_ready"), g)
                rows_of(g)
                masks(g)
                gate_rstd(g - 1)
            gate_rstd(GROUPS - 1)

            gp.wait_ge(sem("resid_added"), 1)
            gp.memset(mask0, 0.0)
            link(gp.memset(mask1, 0.0))
            keep(mask0[:, CH:], [[0, CH]], -CH, 1, NEG)
            keep(mask1[:, 3 * CH:], [[0, CH]], -CH, 1, NEG, "masks_made")

            gp.wait_ge(sem("masks_made"), 1)
            gp.wait_ge(sem("h_ms"), 1)
            rsqrt(h_rs, h_ms, "h_rstd")

            def kq_rstd(count):
                gp.wait_ge(sem("kq_ms"), count)
                rsqrt(kq_rs, kq_ss, "kq_rstd")

            kq_rstd(1)
            with gp.Fori(1, 4) as j:
                kq_rstd(j * 2)
                kq_rstd(j * 2 + 1)
                gp.wait_ge(sem("o_ms"), j)
                rsqrt(o_rs, o_ss, "o_rstd")
            kq_rstd(8)
            gp.wait_ge(sem("o_ms"), 4)
            rsqrt(o_rs, o_ss, "o_rstd")


_INS = ["x", "mlp_norm_w", "w_up", "w_down", "ssm_norm_w", "ssm_w_in", "ssm_conv_w", "ssm_conv_b", "ssm_dt_bias",
        "ssm_a_log", "ssm_d", "ssm_out_norm_w", "ssm_w_out", "kv_norm_w", "w_kv", "k_norm_w", "attn_norm_w", "w_q",
        "q_norm_w", "lam_q1", "lam_k1", "lam_q2", "lam_k2", "subln_w", "w_o"]


def kernel(**inputs):
    import concourse.bacc as bacc
    from concourse.bass_utils import run_bass_kernel_spmd

    nc = bacc.Bacc("TRN2", target_bir_lowering=False, num_devices=1)
    arrays, args = {}, []
    for name in _INS:
        a = np.ascontiguousarray(inputs[name])
        arrays[f"in_{name}"] = a
        args.append(nc.dram_tensor(f"in_{name}", a.shape, mybir.dt.from_np(a.dtype), kind="ExternalInput").ap())
    args.append(nc.dram_tensor("out_0", (1, SEQ, D), F32, kind="ExternalOutput").ap())
    trunk(nc, *args)
    r = run_bass_kernel_spmd(nc, [arrays], core_ids=[0])
    return r.results[0]["out_0"]
```

```python
import math
import numpy as np
import concourse.bass as bass
import concourse.mybir as mybir
from contextlib import ExitStack

F32 = mybir.dt.float32
F32R = mybir.dt.float32r
ALU = mybir.AluOpType
ACT = mybir.ActivationFunctionType
AX = mybir.AxisListType

P = 128
SEQ, D, FF = 256, 2048, 8192
TT = SEQ // P
KT = D // P
NB = 512
INNER, HEADS, HP, GROUPS = 4096, 64, 64, 8
HG = HEADS // GROUPS
GC = INNER // GROUPS
CH = 64
TAPS = 4
CT = (INNER + 2 * GROUPS * P) // P
EPS = 1e-5
HD = 128
LAMBDA_INIT = 0.8 - 0.6 * math.exp(-0.3)
NEG = -1e30

RING = 4
PIECE = 1024

PER_GROUP = 20
IN0 = 1
OUT0 = IN0 + GROUPS * PER_GROUP
UP0 = OUT0 + 4 * 16
PER_CHUNK = 64
ATT0 = UP0 + 4 * PER_CHUNK
PER_PAIR = 24
WO0 = ATT0 + 4 * PER_PAIR
UP1 = WO0 + 4 * 8
PIECES = UP1 + 4 * PER_CHUNK

R_OUT, R_MLP0, R_WO, R_MLP1 = 0, 4, 20, 24
T_OUT, T_MLP0, T_MLP0_END, T_WO, T_MLP1 = 0, 4, 20, 24, 28
ROWS = (2 * CT, 2 * CT, CT, 5 * KT + INNER // P + 4)
ROW_LOADS = 10

WO_ORDER = ([(n, k) for n in (0, 1) for k in range(0, 12, 2)] + [(n, k) for n in (0, 1) for k in (12, 14)]
            + [(n, k) for n in (2, 3) for k in range(0, KT, 2)])

C_CONV, C_CBIAS, C_NORM = 0, TAPS * CT, (TAPS + 1) * CT
N_SSM, N_MLP0, N_MLP1, N_KV, N_ATT, N_OUT = (C_NORM + KT * i for i in range(6))
N_K = N_OUT + INNER // P
N_Q, N_SUB = N_K + 1, N_K + 2
PARAMS = N_SUB + 2


class Pos:

    def __init__(self, c, i=0, m=0):
        self.c, self.i, self.m = c, i, m
        assert m % RING == 0

    def slot(self, off):
        return (self.c + off) % RING

    def done(self, off):
        return self.i * self.m + (self.c + off + 1) if self.m else self.c + off + 1

    def turn(self, off):
        n = (self.c + off) // RING + 1
        return self.i * (self.m // RING) + n if self.m else n


class Chain:

    def __init__(self, eng, sem):
        self.eng, self.sem, self.n, self.base = eng, sem, 0, 0

    def __call__(self, ins):
        ins.then_inc(self.sem, 1)
        self.n += 1
        self.eng.wait_ge(self.sem, self.base + self.n)

    def count(self, ins):
        ins.then_inc(self.sem, 1)
        self.n += 1
        return self.n

    def after(self, n):
        self.eng.wait_ge(self.sem, self.base + n)

    def enter(self, i, first, per):
        self.before = self.n
        self.base, self.n = (i - first) * per + self.before, 0
        self.per = per

    def leave(self, rounds):
        assert self.n == self.per, (self.n, self.per)
        self.base, self.n = 0, self.before + rounds * self.per


def wait(eng, sem, n):
    if not (isinstance(n, int) and n <= 0):
        eng.wait_ge(sem, n)


def col(t, c):
    return t[:, c:c + 1] if isinstance(c, int) else t[:, bass.ds(c, 1)]


def one(c, n):
    return slice(c, c + n) if isinstance(c, int) else bass.ds(c, n)


def one_tile(st, kt, part):
    return st[:, kt, part, :] if isinstance(kt, int) else st[:, bass.ds(kt, 1), part, :].squeeze(1)


def cols3(t, n0, n, c):
    return t[:, n0:n0 + n, one(c, HG)]


def cols(t, c, n):
    return t[:, c:c + n] if isinstance(c, int) else t[:, bass.ds(c, n)]


def trunk(nc, x, mlp_norm_w, w_up, w_down, ssm_norm_w, ssm_w_in, ssm_conv_w, ssm_conv_b, ssm_dt_bias,
          ssm_a_log, ssm_d, ssm_out_norm_w, ssm_w_out, kv_norm_w, w_kv, k_norm_w, attn_norm_w, w_q,
          q_norm_w, lam_q1, lam_k1, lam_q2, lam_k2, subln_w, w_o, out):
    ctx = ExitStack()
    with ctx:
        def sb(name, shape, dt=F32):
            return ctx.enter_context(nc.sbuf_tensor(name, shape, dt))

        sems = {}

        def sem(name):
            if name not in sems:
                sems[name] = ctx.enter_context(nc.semaphore(name))
            return sems[name]

        h = sb("resid", [P, TT, D])
        st = sb("stationary", [P, 3 * KT, 2, SEQ], F32R)
        RA, RB, RC = 0, KT, 2 * KT
        raw = sb("w_raw", [P, RING, PIECE])
        whi = sb("w_hi", [P, RING, PIECE], F32R)
        wlo = sb("w_lo", [P, RING, PIECE], F32R)
        par = sb("params", [P, PARAMS])
        ident = sb("ident", [P, P])
        no_later = sb("no_later", [P, P])
        dt = sb("dt", [P, TT, HEADS])
        dskip = sb("dskip", [P, HEADS])
        colv = sb("colv", [P, 6, HEADS])
        small = sb("small", [P, 66])
        nhalf = small[:, 0:8]
        x_ss, x_rs = small[:, 8:10], small[:, 10:12]
        g_ss, g_ms, g_rs = small[:, 12:14], small[:, 14:16], small[:, 16:18]
        h_ss, h_ms, h_rs = small[:, 18:26], small[:, 26:28], small[:, 28:30]
        kq_ss, kq_rs = small[:, 30:38], small[:, 38:46]
        coef = small[:, 46:54]
        o_ss, o_rs = small[:, 54:58], small[:, 58:62]
        lam_s = small[:, 62:64]
        x_rh = small[:, 64:66]
        arena = sb("work", [P, 10112])

        at = [0]

        def view(n, reset=None):
            if reset is not None:
                at[0] = reset
            v = arena[:, at[0]:at[0] + n]
            at[0] += n
            assert at[0] <= 10112
            return v

        zg = view(1024, 0).rearrange("p (t c) -> p t c", t=TT)
        xraw = view(1024).rearrange("p (t c) -> p t c", t=TT)
        bcraw = view(512).rearrange("p (t c) -> p t c", t=TT)
        bct = view(512).rearrange("p (i t) -> p i t", i=2)
        cvx = view(1024).rearrange("p (i t) -> p i t", i=4)
        th = view(512).rearrange("p (i t) -> p i t", i=2)
        gbuf = view(1024).rearrange("p (t c) -> p t c", t=TT)
        xdt = view(1024).rearrange("p (t c) -> p t c", t=TT)
        m0 = view(2048).rearrange("p (h l) -> p h l", h=HG)
        m1 = view(1024).rearrange("p (h l) -> p h l", h=HG)
        cb = view(384)
        lamv = view(4 * P, 0).rearrange("p (n c) -> p n c", n=4)
        lamt = view(2 * P).rearrange("p (n c) -> p n c", n=2)
        dtT = view(SEQ)
        x_sq = view(D)
        prow = view(4 * P, 5120).rearrange("p (r c) -> p r c", r=4)
        dts = view(8 * 128).rearrange("p (n c) -> p n c", n=8)
        rowsb = view(SEQ)
        kmat = view(5 * P).rearrange("p (n c) -> p n c", n=5)
        da = view(TT * HEADS).rearrange("p (t c) -> p t c", t=TT)
        dtb = view(HEADS)
        alog = view(HEADS)
        act = view(1024, 0).rearrange("p (t c) -> p t c", t=TT)
        pt = arena[:, 0:768].rearrange("p (h q) -> p h q", h=2)
        s0 = view(512).rearrange("p (s k) -> p s k", s=4)
        vall = view(TT * D).rearrange("p (t c) -> p t c", t=TT)
        kq = view(1024).rearrange("p (t c) -> p t c", t=TT)
        kT = view(1024).rearrange("p (s t) -> p s t", s=4)
        qT = view(1024).rearrange("p (s t) -> p s t", s=4)
        s1_at = at[0]
        s1 = view(1024).rearrange("p (s k) -> p s k", s=4)
        ob = arena[:, s1_at:s1_at + 1024].rearrange("p (t c) -> p t c", t=TT)
        mask0, mask1 = view(P), view(SEQ)

        acc = [ctx.enter_context(nc.psum_tensor(f"acc{i}", [P, TT, NB], F32)) for i in range(2)]
        aux = [ctx.enter_context(nc.psum_tensor(f"aux{i}", [P, TT, NB], F32)) for i in range(2)]
        rows_dram = nc.dram_tensor("decay_rows", [HEADS, SEQ], F32).ap()

        conv_w = lambda j, ct: col(par, ct + (C_CONV + j * CT))
        conv_b = lambda ct: col(par, ct + C_CBIAS)
        param = lambda c: col(par, c)

        def to_channels(bank):
            return lambda i, t: bank[:, i // 2, (i % 2) * SEQ + t * P:(i % 2) * SEQ + (t + 1) * P]

        def turned_tile(bank, i):
            return bank[:, i // 2, (i % 2) * SEQ:(i % 2 + 1) * SEQ]

        def whole(bank):
            return bank[:, :, :].rearrange("p a (b t) -> p (a b) t", t=SEQ)

        x_banks = (acc[1], aux[0], aux[1], acc[0])

        block = ctx.enter_context(nc.Block())

        @block.sync
        def _(sp):
            x_v = x[0].rearrange("(t p) c -> p t c", p=P)

            def load(pos, off, parts):
                wait(sp, sem("lo_made"), pos.done(off) - RING)
                dst = raw[:, pos.slot(off), :].rearrange("p (c k n) -> p c k n", c=len(parts), k=parts[0].shape[1])
                for c, src in enumerate(parts):
                    sp.dma_start(dst[:, c], src).then_inc(sem(f"raw_in{pos.slot(off)}"), 32 // len(parts))

            def blocks(pos, off, w, n0, pieces, k0=0):
                if not isinstance(n0, int):
                    sp.to_reg(n0 * 4)
                for j in range(pieces):
                    load(pos, off + j, (w[:, one(k0 + 2 * j, 2), one(n0, NB)],))

            w_in = ssm_w_in[0].rearrange("(k p) n -> p k n", p=P)
            for n in range(4):
                sp.dma_start(h[:, :, n * NB:(n + 1) * NB], x_v[:, :, n * NB:(n + 1) * NB]).then_inc(sem(f"x_in{n}"), 16)
                if n == 1:
                    load(Pos(0), 0, (w_in[:, :, 2 * INNER + 2 * GROUPS * P:],))
            sp.dma_start(dtb, ssm_dt_bias.to_broadcast([P, HEADS])).then_inc(sem("dtb_in"), 16)

            def param_rows():
                flat = lambda v: v.rearrange("(r c) -> r c", c=P)
                sp.dma_start(prow[0:CT, 2, :], flat(ssm_conv_b[0])).then_inc(sem("rows_in"), 16)
                c = KT
                for v, n in ((mlp_norm_w[0], KT), (mlp_norm_w[1], KT), (kv_norm_w, KT), (attn_norm_w[0], KT),
                             (ssm_out_norm_w[0], INNER // P)):
                    sp.dma_start(prow[c:c + n, 3, :], flat(v)).then_inc(sem("rows_in"), 16)
                    c += n

            def group(g, first=False):
                pos = Pos(IN0, g, PER_GROUP)
                for j in range(4):
                    if first and j == 3:
                        param_rows()
                    load(pos, j, [w_in[:, 4 * j:4 * j + 4, one(g * P + (2 * INNER + i * GROUPS * P), P)] for i in range(2)])
                blocks(pos, 4, w_in, g * GC + INNER, 8)
                blocks(pos, 12, w_in, g * GC, 8)

            group(0, True)
            with sp.Fori(1, GROUPS) as g:
                group(g)

            with sp.Fori(0, 4) as n:
                blocks(Pos(OUT0, n, 16), 0, ssm_w_out[0].rearrange("(k p) n -> p k n", p=P), n * NB, 16)

            def mlp(layer, base):
                up = w_up[layer].rearrange("(k p) n -> p k n", p=P)
                down = w_down[layer].rearrange("(k p) n -> p k n", p=P)
                with sp.Fori(0, 4) as c:
                    with sp.Fori(0, 4) as u:
                        blocks(Pos(base, c * 8 + u, 8), 0, up, c * D + u * NB, 8)
                    with sp.Fori(0, 4) as u:
                        blocks(Pos(base + 32, c * 8 + u, 8), 0, down, u * NB, 8, c * KT)

            mlp(0, UP0)
            kv = w_kv.rearrange("(k p) n -> p k n", p=P)
            wq = w_q[0].rearrange("(k p) n -> p k n", p=P)
            with sp.Fori(0, 4) as j:
                pos = Pos(ATT0, j, PER_PAIR)
                blocks(pos, 0, kv, j * NB + D, 8)
                blocks(pos, 8, kv, j * NB, 8)
                blocks(pos, 16, wq, j * NB, 8)
            wo = w_o[0].rearrange("(k p) n -> p k n", p=P)
            for i, (n, kt) in enumerate(WO_ORDER):
                load(Pos(WO0), i, (wo[:, kt:kt + 2, n * NB:(n + 1) * NB],))
            mlp(1, UP1)

            out_v = out[0].rearrange("(t p) c -> p t c", p=P)
            for n in range(3):
                sp.wait_ge(sem("resid_added"), R_MLP1 + 12 + n + 1)
                sp.dma_start(out_v[:, :, n * NB:(n + 1) * NB], h[:, :, n * NB:(n + 1) * NB]).then_inc(sem("stored"), 16)
            for t in range(TT):
                sp.wait_ge(sem("last_added"), t + 1)
                sp.dma_start(out_v[:, t, 3 * NB:], h[:, t, 3 * NB:]).then_inc(sem("stored"), 16)
            sp.wait_ge(sem("stored"), 5 * 16)

        @block.tensor
        def _(pe):
            def piece(pos, off, ps, ncol, kt, first, last):
                pe.wait_ge(sem("lo_made"), pos.done(off))
                tiles = PIECE // ncol
                hi, lo = (v[:, pos.slot(off), :] for v in (whi, wlo))
                if ncol == 2 * P:
                    hi, lo = (v.rearrange("p (c k n) -> p k c n", c=2, k=tiles) for v in (hi, lo))
                else:
                    hi, lo = (v.rearrange("p (k n) -> p k n", k=tiles) for v in (hi, lo))
                for k in range(tiles):
                    start, stop = first and k == 0, last and k == tiles - 1
                    for t in range(TT):
                        xh, xl = (st[:, kt + k, i, t * P:(t + 1) * P] for i in range(2))
                        o = ps[:, t, 0:ncol]
                        pe.matmul(o, xh, hi[:, k], start=start, stop=False)
                        pe.matmul(o, xh, lo[:, k], start=False, stop=False)
                        mm = pe.matmul(o, xl, hi[:, k], start=False, stop=stop)
                mm.then_inc(sem("w_used"), 1)

            def transposes(dst, src, tiles=4):
                for i in range(tiles):
                    for t in range(TT):
                        tr = pe.transpose(dst(i, t), src(i, t), ident[:, :])
                return tr

            pe.wait_ge(sem("ident_made"), 2)
            pe.wait_ge(sem("norm_in"), 16)
            pe.transpose(acc[0][:, 0, 0:KT], prow[0:KT, 3, :], ident[0:KT, 0:KT]).then_inc(sem("norm_turned"), 1)
            def turn_x(i):
                pe.wait_ge(sem(f"x_in{i}"), 16)
                if i == 3:
                    pe.wait_ge(sem("norm_made"), 1)
                transposes(to_channels(x_banks[i]), lambda c, t: h[:, t, (4 * i + c) * P:(4 * i + c + 1) * P]).then_inc(sem("x_turned"), 1)

            def dt_product(i):
                pe.wait_ge(sem("lo_made"), 1)
                pe.wait_ge(sem("x_split"), i + 1)
                o = acc[1][0:HEADS, 0, 0:SEQ]
                for k in range(4 * i, 4 * i + 4):
                    wh, wl = (v[:, 0, k * HEADS:(k + 1) * HEADS] for v in (whi, wlo))
                    pe.matmul(o, wh, st[:, RA + k, 0, :], start=k == 0, stop=False)
                    pe.matmul(o, wl, st[:, RA + k, 0, :], start=False, stop=False)
                    mm = pe.matmul(o, wh, st[:, RA + k, 1, :], start=False, stop=k == KT - 1)
                return mm

            for i in range(4):
                turn_x(i)
            for i in range(4):
                mm = dt_product(i)
            mm.then_inc(sem("w_used"), 1)

            def turn_dt_and_params():
                pe.wait_ge(sem("dtT_made"), 1)
                for t in range(TT):
                    tr = pe.transpose(acc[1][:, 1, t * HEADS:(t + 1) * HEADS], dtT[0:HEADS, t * P:(t + 1) * P], ident[0:HEADS, 0:HEADS])
                tr.then_inc(sem("dt_turned"), 1)
                pe.wait_ge(sem("rows_in"), 16 * ROW_LOADS)
                pe.wait_ge(sem("head_rows_in"), 16 * 3)
                c = 0
                for r, n in enumerate(ROWS):
                    tr = pe.transpose(aux[1][:, 0, c:c + n], prow[0:n, r, :], ident[0:n, 0:n])
                    c += n
                tr.then_inc(sem("par_turned"), 1)

            def turn_x_back(r):
                pe.wait_ge(sem("x_conv"), 2 * r + 2)
                transposes(lambda i, t: aux[1][:, t, i * P:(i + 1) * P],
                           lambda i, t: cvx[:, i, t * P:(t + 1) * P]).then_inc(sem("x_back"), 1)

            def scan(r):
                pe.wait_ge(sem("xdt_made"), r + 1)
                pe.wait_ge(sem("m_made"), r * 2 + 2)
                for k in range(HG):
                    c = slice(k * HP, (k + 1) * HP)
                    pe.matmul(aux[1][:, 0, c], m0[:, k, 0:P], xdt[:, 0, c], start=True, stop=True)
                    pe.matmul(aux[1][:, 1, c], m0[:, k, P:], xdt[:, 0, c], start=True, stop=False)
                    mm = pe.matmul(aux[1][:, 1, c], m1[:, k, :], xdt[:, 1, c], start=False, stop=True)
                mm.then_inc(sem("y_ready"), 1)

            def turn_gated(r):
                pe.wait_ge(sem("g_normed"), r + 1)
                transposes(to_channels(aux[0]), lambda i, t: gbuf[:, t, i * P:(i + 1) * P]).then_inc(sem("g_turned"), 1)

            def decays():
                pe.wait_ge(sem("kmat_made"), 1)
                pe.wait_ge(sem("da_made"), 1)
                for t in range(TT):
                    pe.matmul(aux[1][0:HEADS, 0, t * P:(t + 1) * P], da[:, t, :], kmat[:, 4, :], start=True, stop=True)
                o = lambda n: aux[1][:, 1, n * HEADS:(n + 1) * HEADS]
                pe.matmul(o(3), kmat[:, 2, :], da[:, 0, :], start=True, stop=False)
                pe.matmul(o(3), kmat[:, 3, :], da[:, 1, :], start=False, stop=True)
                for n, k, t in ((0, 0, 0), (1, 1, 0), (2, 2, 0), (4, 0, 1), (5, 1, 1)):
                    mm = pe.matmul(o(n), kmat[:, k, :], da[:, t, :], start=True, stop=True)
                mm.then_inc(sem("decays_ready"), 1)

            def group(g, first):
                pos = Pos(IN0, g, PER_GROUP)
                for j in range(PER_GROUP):
                    if j == 4 and not first:
                        pe.wait_ge(sem("x_read"), g)
                    if j == 12:
                        if first:
                            pe.wait_ge(sem("dt_read"), 1)
                        else:
                            pe.wait_ge(sem("z_read"), g)
                    if j < 4:
                        piece(pos, j, aux[0], 2 * P, RA + 4 * j, j == 0, j == 3)
                    elif j < 12:
                        piece(pos, j, acc[0], NB, RA + 2 * (j - 4), j == 4, j == 11)
                    else:
                        piece(pos, j, acc[1], NB, RA + 2 * (j - 12), j == 12, j == 19)
                    if j == 2 and not first:
                        turn_x_back(g - 1)
                    if j == 1 and first:
                        turn_dt_and_params()
                    if j == 6 and first:
                        pe.wait_ge(sem("par_made"), 2)
                        decays()
                    if j == 5:
                        pe.wait_ge(sem("bc_read"), g + 1)
                        transposes(lambda i, t: aux[0][:, 0, i * SEQ + t * P:i * SEQ + (t + 1) * P],
                                   lambda i, t: bcraw[:, t, i * P:(i + 1) * P], 2).then_inc(sem("bc_turned"), 1)
                    if j == 7 and not first:
                        scan(g - 1)
                    if j == 10:
                        pe.wait_ge(sem("bc_conv"), g + 1)
                        b, c = bct[:, 0, :], bct[:, 1, :]
                        pe.matmul(aux[0][:, 1, 0:SEQ], b[:, 0:P], c, start=True, stop=True)
                        pe.matmul(aux[0][:, 1, SEQ:SEQ + P], b[:, P:], c[:, P:], start=True, stop=True).then_inc(sem("cb_ready"), 1)
                    if j == 13:
                        pe.wait_ge(sem("x_read"), g + 1)
                        if first:
                            pe.wait_ge(sem("decays_read"), 1)
                        else:
                            pe.wait_ge(sem("y_read"), g)
                        transposes(to_channels(aux[1]), lambda i, t: xraw[:, t, i * P:(i + 1) * P]).then_inc(sem("x_raw_turned"), 1)
                    if j == 15 and not first:
                        pe.wait_ge(sem("cb_read"), g + 1)
                        turn_gated(g - 1)

            group(0, True)
            with pe.Fori(1, GROUPS) as g:
                group(g, False)

            def turn_resid(n, added, turned):
                pe.wait_ge(sem("resid_added"), added)
                transposes(to_channels(aux[n % 2]), lambda i, t: h[:, t, n * NB + i * P:n * NB + (i + 1) * P]).then_inc(sem("turned"), 1)

            for n in range(4):
                for j in range(16):
                    if n == 0 and j == 0:
                        pe.wait_ge(sem("gate_lo"), GROUPS - 1)
                        pe.wait_ge(sem("x_read"), GROUPS)
                    if n == 0 and j == 14:
                        pe.wait_ge(sem("gate_lo"), GROUPS)
                    if n == 1 and j == 0:
                        pe.wait_ge(sem("z_read"), GROUPS)
                    if n >= 2 and j == 0:
                        pe.wait_ge(sem("resid_added"), n - 1)
                    piece(Pos(OUT0), 16 * n + j, acc[n % 2], NB, RB + 2 * j, j == 0, j == 15)
                    if n == 0 and j == 2:
                        turn_x_back(GROUPS - 1)
                    if n == 0 and j == 7:
                        scan(GROUPS - 1)
                    if n == 0 and j == 12:
                        pe.wait_ge(sem("cb_read"), GROUPS)
                        turn_gated(GROUPS - 1)
                    if n >= 1 and j == 2:
                        if n == 2:
                            pe.wait_ge(sem("y_read"), GROUPS)
                        if n == 3:
                            pe.wait_ge(sem("turned_lo"), 1)
                        turn_resid(n - 1, R_OUT + n, T_OUT + n)

            def mlp(base, R, T, U, T_carry):
                def up(c, u, fresh=False):
                    pos = Pos(base, c, PER_CHUNK)
                    off = 8 * u
                    for j in range(8):
                        if j == 0:
                            if u < 2:
                                pe.wait_ge(sem("resid_added"), c * 4 + (R - 1 + u))
                            else:
                                pe.wait_ge(sem("up_read"), c * 4 + (U + u - 1))
                            if fresh:
                                pe.wait_ge(sem("turned_lo"), T - 1)
                        if j == 6 and fresh:
                            pe.wait_ge(sem("turned_lo"), T)
                        piece(pos, off + j, acc[u % 2], NB, RA + 2 * j, j == 0, j == 7)
                        if j == 2 and fresh:
                            wait(pe, sem("turned_lo"), T - 2)
                            turn_resid(3, R, T)
                        if j == 2 and u > 0:
                            turn_up(c, u - 1)

                def turn_up(c, u):
                    pe.wait_ge(sem("up_read"), c * 4 + (U + u + 1))
                    pe.wait_ge(sem("turned_lo"), c * 4 + (T + u - 1))
                    transposes(to_channels(aux[u % 2]), lambda i, t: act[:, t, i * P:(i + 1) * P]).then_inc(sem("turned"), 1)

                def down(c, d, carry):
                    pos = Pos(base, c, PER_CHUNK)
                    for j in range(8):
                        if j == 0:
                            if d < 2:
                                pe.wait_ge(sem("up_read"), c * 4 + (U + 3 + d))
                            else:
                                pe.wait_ge(sem("resid_added"), c * 4 + (R + d - 1))
                            if d == 0:
                                pe.wait_ge(sem("turned_lo"), c * 4 + (T + 3))
                        if j == 6 and d == 0:
                            pe.wait_ge(sem("turned_lo"), c * 4 + (T + 4))
                        piece(pos, 32 + 8 * d + j, acc[d % 2], NB, RB + 2 * j, j == 0, j == 7)
                        if j == 2 and d == 0:
                            turn_up(c, 3)
                        if j == 2 and d > 0 and carry:
                            pe.wait_ge(sem("turned_lo"), T_carry + d - 2)
                            turn_resid(d - 1, c * 4 + (R + d), None)

                up(0, 0, True)
                with pe.Fori(0, 3) as c:
                    for u in range(1, 4):
                        up(c, u)
                    for d in range(4):
                        down(c, d, False)
                    up(c + 1, 0)
                for u in range(1, 4):
                    up(3, u)
                for d in range(4):
                    down(3, d, T_carry is not None)

            mlp(UP0, R_MLP0, T_MLP0, 0, T_MLP0_END)

            def turn_q(r):
                pe.wait_ge(sem("q_normed"), r + 1)
                pe.wait_ge(sem("kT_made"), r + 1)
                transposes(to_channels(aux[1]), lambda i, t: kq[:, t, i * P:(i + 1) * P]).then_inc(sem("q_turned"), 1)

            def scores_a(r):
                pe.wait_ge(sem("qT_made"), r + 1)
                for s in range(4):
                    pe.matmul(aux[1][:, 0, s * P:(s + 1) * P], qT[:, s, 0:P], kT[:, s, 0:P], start=True, stop=True)
                for s in range(2):
                    mm = pe.matmul(aux[1][:, 1, s * SEQ:(s + 1) * SEQ], qT[:, s, P:], kT[:, s, :], start=True, stop=True)
                mm.then_inc(sem("sa_ready"), 1)

            def scores_b(r):
                for s in range(2):
                    mm = pe.matmul(aux[0][:, 0, s * SEQ:(s + 1) * SEQ], qT[:, 2 + s, P:], kT[:, 2 + s, :], start=True, stop=True)
                mm.then_inc(sem("sb_ready"), 1)

            def turn_p(r):
                pe.wait_ge(sem("p_made"), r + 1)
                for k in range(2):
                    pe.transpose(aux[1][:, k, 0:P], s0[:, 2 * k, :], ident[:, :])
                    for i in range(2):
                        tr = pe.transpose(aux[1][:, k, (1 + i) * P:(2 + i) * P], s1[:, 2 * k, i * P:(i + 1) * P], ident[:, :])
                tr.then_inc(sem("p_turned"), 1)

            def apply_p(r):
                pe.wait_ge(sem("pt_made"), r + 1)
                for k in range(2):
                    v = [cols(vall[:, t, :], r * NB + k * 2 * HD, 2 * HD) for t in range(TT)]
                    o = slice(k * 2 * HD, (k + 1) * 2 * HD)
                    pe.matmul(aux[0][:, 0, o], pt[:, k, 0:P], v[0], start=True, stop=True)
                    pe.matmul(aux[0][:, 1, o], pt[:, k, P:2 * P], v[0], start=True, stop=False)
                    mm = pe.matmul(aux[0][:, 1, o], pt[:, k, 2 * P:], v[1], start=False, stop=True)
                mm.then_inc(sem("o_ready"), 1)

            def turn_o(r):
                pe.wait_ge(sem("o_normed"), r + 1)
                transposes(to_channels(aux[0]), lambda i, t: ob[:, t, i * P:(i + 1) * P]).then_inc(sem("o_turned"), 1)

            def pair(j, first):
                pos = Pos(ATT0, j, PER_PAIR)
                for i in range(PER_PAIR):
                    if first:
                        if i == 0:
                            pe.wait_ge(sem("turned_lo"), T_MLP0_END + 3)
                        if i == 6:
                            pe.wait_ge(sem("turned_lo"), T_MLP0_END + 4)
                        if i == 8:
                            pe.wait_ge(sem("resid_added"), R_WO - 1)
                        if i == 16:
                            pe.wait_ge(sem("resid_added"), R_WO)
                    else:
                        if i == 8:
                            pe.wait_ge(sem("k_read"), j)
                        if i == 16:
                            pe.wait_ge(sem("q_read"), j)
                    ps, region = ((aux[0], RA), (acc[0], RA), (acc[1], RC))[i // 8]
                    piece(pos, i, ps, NB, region + 2 * (i % 8), i % 8 == 0, i % 8 == 7)
                    if i == 2 and first:
                        turn_resid(3, R_WO, None)
                    if i == 22:
                        pe.wait_ge(sem("k_normed"), j + 1)
                        if not first:
                            pe.wait_ge(sem("pt_made"), j)
                        transposes(to_channels(aux[1]), lambda c, t: kq[:, t, c * P:(c + 1) * P]).then_inc(sem("k_turned"), 1)
                    if not first:
                        if i == 4:
                            turn_q(j - 1)
                        if i == 7:
                            scores_a(j - 1)
                        if i == 9:
                            pe.wait_ge(sem("v_read"), j + 1)
                            scores_b(j - 1)
                        if i == 15:
                            turn_p(j - 1)
                        if i == 16:
                            apply_p(j - 1)
                        if i == 20:
                            turn_o(j - 1)

            pair(0, True)
            with pe.Fori(1, 4) as j:
                pair(j, False)

            for i, (n, kt) in enumerate(WO_ORDER):
                if i == 0:
                    pe.wait_ge(sem("o_lo"), 3)
                    pe.wait_ge(sem("k_read"), 4)
                if i == 6:
                    pe.wait_ge(sem("q_read"), 4)
                if i == 12:
                    pe.wait_ge(sem("o_lo"), 4)
                if i == 16:
                    pe.wait_ge(sem("resid_added"), R_WO + 1)
                if i == 24:
                    pe.wait_ge(sem("resid_added"), R_WO + 2)
                piece(Pos(WO0), i, acc[n % 2], NB, RB + kt, kt == 0, kt == KT - 2)
                if i == 2:
                    turn_q(3)
                if i == 3:
                    scores_a(3)
                    scores_b(3)
                if i == 7:
                    turn_p(3)
                if i == 8:
                    apply_p(3)
                if i == 10:
                    turn_o(3)
                if i == 17:
                    turn_resid(0, R_WO + 1, None)
                if i == 19:
                    turn_resid(1, R_WO + 2, None)
                if i == 26:
                    pe.wait_ge(sem("turned_lo"), T_WO + 1)
                    turn_resid(2, R_WO + 3, None)

            mlp(UP1, R_MLP1, T_MLP1, 16, None)

        @block.scalar
        def _(act_e):
            a = act_e
            taps = ssm_conv_w[0].rearrange("j (r c) -> j r c", c=P)
            a.dma_start(prow[0:KT, 3, :], ssm_norm_w[0].rearrange("(r c) -> r c", c=P)).then_inc(sem("norm_in"), 16)
            for r in range(2):
                for j in range(2):
                    a.dma_start(prow[j * CT:(j + 1) * CT, r, :], taps[2 * r + j]).then_inc(sem("rows_in"), 16)
            def hi(pos, off):
                a.wait_ge(sem(f"raw_in{pos.slot(off)}"), pos.turn(off) * 32)
                wait(a, sem("w_used"), pos.done(off) - RING)
                s = pos.slot(off)
                a.activation(whi[:, s, :], raw[:, s, :], ACT.Copy).then_inc(sem("hi_made"), 1)

            def split_hi(bank, kt, w):
                for i in range(4):
                    ins = a.activation(st[:, kt + i, 0, :] if isinstance(kt, int) else st[:, bass.ds(kt + i, 1), 0, :],
                                       turned_tile(bank, i), ACT.Copy, scale=param(w + i))
                return ins

            a.wait_ge(sem("norm_turned"), 1)
            a.activation(par[:, N_SSM:N_SSM + KT], acc[0][:, 0, 0:KT], ACT.Copy).then_inc(sem("norm_made"), 1)
            a.wait_ge(sem("norm_made"), 1)
            for i, bank in enumerate(x_banks):
                a.wait_ge(sem("x_turned"), i + 1)
                split_hi(bank, RA + 4 * i, N_SSM + 4 * i).then_inc(sem("x_hi"), 1)
                if i == 1:
                    hi(Pos(0), 0)

            def x_squares(t):
                if t:
                    a.wait_ge(sem("x_squared"), t)
                a.activation(x_sq, h[:, t, :], ACT.Square, accum_out=x_ss[:, t:t + 1]).then_inc(sem("x_squared"), 1)

            def start(j):
                if j == 0:
                    x_squares(0)
                if j == 1:
                    x_squares(1)
                    a.wait_ge(sem("w_used"), 1)
                    a.activation(dtT[0:HEADS, :], acc[1][0:HEADS, 0, 0:SEQ], ACT.Copy).then_inc(sem("dtT_made"), 1)
                if j == 2:
                    a.wait_ge(sem("alog_in"), 16)
                    a.activation(alog, alog, ACT.Exp).then_inc(sem("a_made"), 1)
                if j == 3:
                    a.wait_ge(sem("dt_abs"), 1)
                    a.activation(dts[:, 2, :], dts[:, 1, :], ACT.Exp, scale=-1.0).then_inc(sem("dt_exp"), 1)
                if j == 4:
                    a.wait_ge(sem("par_turned"), 1)
                    a.activation(par[:, 0:C_NORM], aux[1][:, 0, 0:C_NORM], ACT.Copy, scale=0.5)
                    a.activation(par[:, N_MLP0:N_SUB], aux[1][:, 0, N_MLP0:N_SUB], ACT.Copy).then_inc(sem("par_made"), 1)
                    a.activation(par[:, N_SUB:], aux[1][:, 0, N_SUB:PARAMS], ACT.Copy, scale=1.0 - LAMBDA_INIT).then_inc(sem("par_made"), 1)
                if j == 11:
                    a.wait_ge(sem("lam_summed"), 1)
                    a.activation(lam_s, lam_s, ACT.Exp).then_inc(sem("lam_exp"), 1)
                if j == 8:
                    a.wait_ge(sem("decays_ready"), 1)
                    a.activation(rowsb[0:HEADS, :], aux[1][0:HEADS, 0, 0:SEQ], ACT.Copy).then_inc(sem("rows_made"), 1)
                    a.activation(colv[:, :, :].rearrange("p n h -> p (n h)"), aux[1][:, 1, 0:6 * HEADS], ACT.Copy).then_inc(sem("decays_read"), 1)

            def tail(j, r, end):
                if j == 0:
                    a.wait_ge(sem("masked"), r * 2 + 2)
                    a.activation(m0, m0, ACT.Exp).then_inc(sem("decay_made"), 1)
                if j == 1:
                    a.wait_ge(sem("x_conv_lin"), r * 4 + 4)
                    a.wait_ge(sem("x_conv"), r * 2 + 1)
                    a.activation(th, cvx[:, 2:4, :], ACT.Tanh).then_inc(sem("x_tanh"), 1)
                if j == 3:
                    a.wait_ge(sem("w_used"), Pos(IN0, r, PER_GROUP).done(19))
                    wait(a, sem("gated"), r)
                    for t in range(TT):
                        ins = a.activation(zg[:, t, :], acc[1][:, t, :], ACT.Tanh, scale=x_rh[:, t:t + 1])
                    ins.then_inc(sem("z_tanh"), 1)
                if j == 12:
                    a.wait_ge(sem("gated"), r + 1)
                    for t in range(TT):
                        ins = a.activation(xraw[:, t, :], gbuf[:, t, :], ACT.Square, accum_out=g_ss[:, t:t + 1])
                    ins.then_inc(sem("g_squared"), 1)
                if j == 14:
                    a.wait_ge(sem("g_rstd"), r + 1)
                    for t in range(TT):
                        ins = a.activation(gbuf[:, t, :], gbuf[:, t, :], ACT.Copy, scale=g_rs[:, t:t + 1])
                    ins.then_inc(sem("g_normed"), 1)
                if j == end:
                    a.wait_ge(sem("g_turned"), r + 1)
                    split_hi(aux[0], r * 4 + RB, r * 4 + N_OUT).then_inc(sem("gate_hi"), 1)

            def read_x_product(dst, ps, n):
                for t in range(TT):
                    ins = a.activation(dst[:, t, :], ps[:, t, 0:n], ACT.Copy, scale=x_rs[:, t:t + 1])
                return ins

            def group(g, first):
                pos = Pos(IN0, g, PER_GROUP)
                for j in range(PER_GROUP):
                    hi(pos, j)
                    if first:
                        start(j)
                    if j == 7:
                        if first:
                            a.wait_ge(sem("x_rstd"), 1)
                        a.wait_ge(sem("w_used"), pos.done(3))
                        read_x_product(bcraw, aux[0], 2 * P).then_inc(sem("bc_read"), 1)
                    if j == 9:
                        a.wait_ge(sem("bc_turned"), g + 1)
                        for i in range(2):
                            ct = g + (INNER // P + i * GROUPS)
                            ins = a.activation(bct[:, i, :], aux[0][:, 0, i * SEQ:(i + 1) * SEQ], ACT.Identity,
                                               bias=conv_b(ct), scale=conv_w(3, ct))
                        ins.then_inc(sem("bc_tap"), 1)
                    if j == 10:
                        a.wait_ge(sem("bc_conv_lin"), g + 1)
                        if not first:
                            a.wait_ge(sem("x_conv"), g * 2)
                        a.activation(th, bct, ACT.Tanh).then_inc(sem("bc_tanh"), 1)
                    if not first:
                        tail(j, g - 1, 19)
                    if j == 14:
                        a.wait_ge(sem("cb_ready"), g + 1)
                        if not first:
                            a.wait_ge(sem("m_made"), g * 2)
                        a.activation(cb, aux[0][:, 1, 0:3 * P], ACT.Copy).then_inc(sem("cb_read"), 1)
                    if j == 15:
                        a.wait_ge(sem("w_used"), pos.done(11))
                        if not first:
                            a.wait_ge(sem("g_squared"), g)
                        read_x_product(xraw, acc[0], NB).then_inc(sem("x_read"), 1)
                    if j == 17:
                        a.wait_ge(sem("x_raw_turned"), g + 1)
                        for i in range(4):
                            ct = g * 4 + i
                            a.activation(cvx[:, i, :], turned_tile(aux[1], i), ACT.Identity,
                                         bias=conv_b(ct), scale=conv_w(3, ct)).then_inc(sem("x_tap"), 1)
                    if j == 18:
                        a.wait_ge(sem("masked"), g * 2 + 1)
                        a.activation(m1, m1, ACT.Exp).then_inc(sem("decay_made"), 1)
                    if j == 19:
                        a.wait_ge(sem("x_conv_lin"), g * 4 + 2)
                        a.wait_ge(sem("bc_conv"), g + 1)
                        a.activation(th, cvx[:, 0:2, :], ACT.Tanh).then_inc(sem("x_tanh"), 1)

            group(0, True)
            with a.Fori(1, GROUPS) as g:
                group(g, False)

            squared = [0]

            def resid_squares(n, added):
                a.wait_ge(sem("resid_added"), added)
                wait(a, sem("h_squared"), squared[0])
                squared[0] += 1
                for t in range(TT):
                    ins = a.activation(act[:, t, :], h[:, t, n * NB:(n + 1) * NB], ACT.Square, accum_out=h_ss[:, t * 4 + n:t * 4 + n + 1])
                ins.then_inc(sem("h_squared"), 1)

            def resid_hi(n, turned, targets):
                a.wait_ge(sem("turned"), turned)
                for region, w in targets:
                    ins = split_hi(aux[n % 2], region + 4 * n, w + 4 * n)
                ins.then_inc(sem("turned_hi"), 1)

            to_mlp0, to_att, to_mlp1 = [(RA, N_MLP0)], [(RA, N_KV), (RC, N_ATT)], [(RA, N_MLP1)]

            for n in range(4):
                for j in range(16):
                    hi(Pos(OUT0), 16 * n + j)
                    if n == 0:
                        tail(j, GROUPS - 1, 15)
                    if n >= 1 and j == 3:
                        resid_squares(n - 1, R_OUT + n)
                    if n >= 1 and j == 5:
                        resid_hi(n - 1, T_OUT + n, to_mlp0)

            def mlp(base, R, T, U, T_carry, before, after):
                def relu(c, u):
                    a.wait_ge(sem("w_used"), Pos(base, c, PER_CHUNK).done(8 * u + 7))
                    if u > 0:
                        a.wait_ge(sem("turned"), c * 4 + (T + u))
                    else:
                        a.wait_ge(sem("turned"), c * 4 + T)
                        a.wait_ge(sem("h_squared"), squared[0])
                    a.activation(act, acc[u % 2][:, :, :], ACT.Relu).then_inc(sem("relu_made"), 1)

                def up_hi(c, u):
                    a.wait_ge(sem("turned"), c * 4 + (T + u + 1))
                    a.activation(st[:, RB + 4 * u:RB + 4 * u + 4, 0, :], whole(aux[u % 2]), ACT.Copy).then_inc(sem("turned_hi"), 1)

                def run(c, off, steps):
                    for j in range(8):
                        hi(Pos(base, c, PER_CHUNK), off + j)
                        steps(j)

                def after_up(c, u):
                    def steps(j):
                        if j == 2:
                            relu(c, u)
                        if j == 5:
                            up_hi(c, u)
                    return steps

                def after_resid(n, added, turned, targets):
                    def steps(j):
                        if j == 3 and targets:
                            resid_squares(n, added)
                        if j == 5 and targets:
                            resid_hi(n, turned, targets)
                    return steps

                run(0, 0, after_resid(3, R, T, before))
                with a.Fori(0, 3) as c:
                    for u in range(1, 5):
                        run(c, 8 * u, after_up(c, u - 1))
                    for d in range(1, 5):
                        run(c, 32 + 8 * d, after_resid(d - 1, None, None, None))
                for u in range(1, 5):
                    run(3, 8 * u, after_up(3, u - 1))
                for d in range(1, 4):
                    run(3, 32 + 8 * d, after_resid(d - 1, R + 12 + d, (T_carry or 0) + d, after))

            mlp(UP0, R_MLP0, T_MLP0, 0, T_MLP0_END, to_mlp0, to_att)

            def read_scaled(dst, ps):
                for t in range(TT):
                    ins = a.activation(dst(t), ps[:, t, :], ACT.Copy, scale=h_rs[:, t:t + 1])
                return ins

            def read_q(r):
                a.wait_ge(sem("w_used"), Pos(ATT0, r, PER_PAIR).done(23))
                a.wait_ge(sem("k_turned"), r + 1)
                read_scaled(lambda t: kq[:, t, :], acc[1]).then_inc(sem("q_read"), 1)

            def make_kT(r):
                a.wait_ge(sem("k_turned"), r + 1)
                a.activation(kT, whole(aux[1]), ACT.Copy, scale=param(N_K)).then_inc(sem("kT_made"), 1)

            def make_qT(r):
                a.wait_ge(sem("q_turned"), r + 1)
                a.activation(qT, whole(aux[1]), ACT.Copy, scale=param(N_Q)).then_inc(sem("qT_made"), 1)

            def exps(r, t):
                a.wait_ge(sem("max_made"), r * 2 + (t + 1))
                for s in range(4):
                    v = (s0, s1)[t][:, s, :]
                    n = t * 4 + s
                    ins = a.activation(v, v, ACT.Exp, bias=kq_ss[:, n:n + 1], scale=HD ** -0.5, accum_out=kq_rs[:, n:n + 1])
                ins.then_inc(sem("exp_made"), 1)

            def make_pt(r):
                a.wait_ge(sem("p_turned"), r + 1)
                a.activation(pt, aux[1][:, :, 0:3 * P], ACT.Copy).then_inc(sem("pt_made"), 1)

            def o_squares(r):
                a.wait_ge(sem("o_ready"), r + 1)
                for t in range(TT):
                    for k in range(2):
                        o = slice(k * 2 * HD, (k + 1) * 2 * HD)
                        n = t * 2 + k
                        ins = a.activation(ob[:, t, o], aux[0][:, t, o], ACT.Square, accum_out=o_ss[:, n:n + 1])
                ins.then_inc(sem("o_squared"), 1)

            def o_norm(r):
                a.wait_ge(sem("o_rstd"), r + 1)
                for t in range(TT):
                    for k in range(2):
                        o = slice(k * 2 * HD, (k + 1) * 2 * HD)
                        n = t * 2 + k
                        ins = a.activation(ob[:, t, o], aux[0][:, t, o], ACT.Copy, scale=o_rs[:, n:n + 1])
                ins.then_inc(sem("o_normed"), 1)

            def o_hi(r):
                a.wait_ge(sem("o_turned"), r + 1)
                for i in range(4):
                    ins = a.activation(one_tile(st, r * 4 + (RB + i), 0), turned_tile(aux[0], i), ACT.Copy, scale=param(N_SUB + i % 2))
                ins.then_inc(sem("o_hi"), 1)

            def pair(j, first):
                pos = Pos(ATT0, j, PER_PAIR)
                for i in range(PER_PAIR):
                    hi(pos, i)
                    if first and i == 3:
                        resid_squares(3, R_WO)
                    if first and i == 5:
                        resid_hi(3, T_MLP0_END + 4, to_att)
                    if i == 11:
                        if first:
                            a.wait_ge(sem("h_rstd"), 1)
                        a.wait_ge(sem("w_used"), pos.done(7))
                        read_scaled(lambda t: cols(vall[:, t, :], j * NB, NB), aux[0]).then_inc(sem("v_read"), 1)
                    if not first:
                        r = j - 1
                        if i == 1:
                            make_kT(r)
                        if i == 3:
                            read_q(r)
                        if i == 8:
                            make_qT(r)
                        if i == 14:
                            exps(r, 0)
                        if i == 15:
                            exps(r, 1)
                        if i == 18:
                            make_pt(r)
                        if i == 20:
                            o_squares(r)
                        if i == 21:
                            o_norm(r)
                        if i == 23:
                            o_hi(r)
                    if i == 19:
                        a.wait_ge(sem("w_used"), pos.done(15))
                        if not first:
                            a.wait_ge(sem("q_turned"), j)
                        read_scaled(lambda t: kq[:, t, :], acc[0]).then_inc(sem("k_read"), 1)

            pair(0, True)
            with a.Fori(1, 4) as j:
                pair(j, False)

            for i in range(len(WO_ORDER)):
                hi(Pos(WO0), i)
                if i == 1:
                    make_kT(3)
                if i == 2:
                    read_q(3)
                if i == 5:
                    make_qT(3)
                if i == 7:
                    exps(3, 0)
                    exps(3, 1)
                if i == 9:
                    make_pt(3)
                if i == 12:
                    o_squares(3)
                    o_norm(3)
                if i == 13:
                    o_hi(3)
                for n, at_sq, at_hi in ((0, 17, 20), (1, 19, 22), (2, 27, 29)):
                    if i == at_sq:
                        resid_squares(n, R_WO + n + 1)
                    if i == at_hi:
                        resid_hi(n, T_WO + n + 1, to_mlp1)

            mlp(UP1, R_MLP1, T_MLP1, 16, None, to_mlp1, None)

        @block.vector
        def _(v):
            link = Chain(v, sem("v_chain"))

            def lo(pos, off):
                v.wait_ge(sem("hi_made"), pos.done(off))
                s = pos.slot(off)
                v.tensor_tensor(wlo[:, s, :], raw[:, s, :], whi[:, s, :].bitcast(F32), ALU.subtract).then_inc(sem("lo_made"), 1)

            def split_lo(bank, kt, w):
                for i in range(4):
                    ins = v.scalar_tensor_tensor(one_tile(st, kt + i, 1), turned_tile(bank, i), param(w + i),
                                                 one_tile(st, kt + i, 0).bitcast(F32), ALU.mult, ALU.subtract)
                return ins

            def mean_eps(out, sums, n, eps):
                return v.tensor_scalar(out, sums, 1.0 / n, eps, ALU.mult, ALU.add)

            for i, bank in enumerate(x_banks):
                v.wait_ge(sem("x_hi"), i + 1)
                split_lo(bank, RA + 4 * i, N_SSM + 4 * i).then_inc(sem("x_split"), 1)
                if i == 1:
                    lo(Pos(0), 0)

            def lambda_sums():
                v.wait_ge(sem("lam_in"), 4 * 16)
                for i in range(2):
                    last = v.tensor_tensor(lamt[:, i, :], lamv[:, 2 * i, :], lamv[:, 2 * i + 1, :], ALU.mult)
                link(last)
                v.tensor_reduce(lam_s, lamt, AX.X, ALU.add).then_inc(sem("lam_summed"), 1)
                link(v.memset(coef, 1.0))

            def lambda_coef():
                v.wait_ge(sem("lam_exp"), 1)
                minus_lam = coef.rearrange("p (a b) -> p a b", b=2)[:, :, 1]
                link(v.scalar_tensor_tensor(lam_s[:, 0:1], lam_s[:, 1:2], LAMBDA_INIT, lam_s[:, 0:1], ALU.subtract, ALU.subtract))
                link(v.tensor_copy(minus_lam, lam_s[:, 0:1].to_broadcast([P, 4])))

            def start(j):
                tm = lambda i: dts[:, i, :]
                if j == 1:
                    v.wait_ge(sem("x_squared"), TT)
                    mean_eps(x_ss, x_ss, D, EPS).then_inc(sem("x_ms"), 1)
                if j == 2:
                    v.wait_ge(sem("x_rstd"), 1)
                    v.wait_ge(sem("dt_turned"), 1)
                    v.wait_ge(sem("dtb_in"), 16)
                    v.tensor_scalar(x_rh, x_rs, 0.5, None, ALU.mult)
                    for t in range(TT):
                        n = slice(t * HEADS, (t + 1) * HEADS)
                        ins = v.scalar_tensor_tensor(dts[:, 0, n], acc[1][:, 1, n], x_rs[:, t:t + 1], dtb, ALU.mult, ALU.add)
                    ins.then_inc(sem("dt_read"), 1)
                    v.wait_ge(sem("dt_read"), 1)
                    v.scalar_tensor_tensor(tm(1), tm(0), -1.0, tm(0), ALU.mult, ALU.max).then_inc(sem("dt_abs"), 1)
                if j == 3:
                    v.wait_ge(sem("dt_exp"), 1)
                    link(v.tensor_scalar(tm(3), tm(2), 2.0, None, ALU.add))
                    link(v.reciprocal(tm(4), tm(3)))
                if j == 4:
                    link(v.tensor_tensor(tm(5), tm(2), tm(4), ALU.mult))
                    link(v.tensor_tensor(tm(6), tm(5), tm(5), ALU.mult))
                    link(v.tensor_scalar(tm(7), tm(6), 1.0 / 17, None, ALU.mult))
                    link(v.scalar_tensor_tensor(tm(7), tm(7), 1.0 / 15, tm(6), ALU.add, ALU.mult))
                if j == 5:
                    for n in (13, 11, 9):
                        link(v.scalar_tensor_tensor(tm(7), tm(7), 1.0 / n, tm(6), ALU.add, ALU.mult))
                if j == 6:
                    for n in (7, 5, 3):
                        link(v.scalar_tensor_tensor(tm(7), tm(7), 1.0 / n, tm(6), ALU.add, ALU.mult))
                if j == 7:
                    link(v.scalar_tensor_tensor(tm(7), tm(7), 1.0, tm(5), ALU.add, ALU.mult))
                    link(v.tensor_scalar(tm(1), tm(0), 0.0, None, ALU.max))
                    link(v.scalar_tensor_tensor(dt[:, :, :].rearrange("p t h -> p (t h)"), tm(7), 2.0, tm(1), ALU.mult, ALU.add))
                    v.wait_ge(sem("a_made"), 1)
                    v.scalar_tensor_tensor(da, dt[:, :, :], -1.0, alog.unsqueeze(1).to_broadcast([P, TT, HEADS]),
                                           ALU.mult, ALU.mult).then_inc(sem("da_made"), 1)
                if j == 8:
                    lambda_sums()
                if j == 12:
                    lambda_coef()

            def conv(pairs):
                made, last = [0, 0], [None, None]
                for sh in range(1, TAPS):
                    for i, (dst, src, ct) in enumerate(pairs):
                        if sh > 1:
                            link.after(made[i])
                        last[i] = v.scalar_tensor_tensor(dst[:, sh:], src[:, 0:SEQ - sh], conv_w(TAPS - 1 - sh, ct), dst[:, sh:], ALU.mult, ALU.add)
                        if sh < TAPS - 1:
                            made[i] = link.count(last[i])
                return last

            def conv_x(r, i0):
                v.wait_ge(sem("x_tap"), r * 4 + (i0 + 2))
                for ins in conv([(cvx[:, i, :], turned_tile(aux[1], i), r * 4 + i) for i in (i0, i0 + 1)]):
                    ins.then_inc(sem("x_conv_lin"), 1)

            def by_head(table, r):
                return cols(table, r * HG, HG).unsqueeze(2).to_broadcast([P, HG, HP])

            heads = lambda ap: ap.rearrange("p (h c) -> p h c", h=HG)

            def tail(j, r, end):
                if j == 0:
                    v.wait_ge(sem("x_tanh"), r * 2 + 1)
                    v.scalar_tensor_tensor(cvx[:, 0:2, :], th, 1.0, cvx[:, 0:2, :], ALU.add, ALU.mult).then_inc(sem("x_conv"), 1)
                if j == 2:
                    v.wait_ge(sem("x_tanh"), r * 2 + 2)
                    v.scalar_tensor_tensor(cvx[:, 2:4, :], th, 1.0, cvx[:, 2:4, :], ALU.add, ALU.mult).then_inc(sem("x_conv"), 1)
                if j == 4:
                    v.wait_ge(sem("z_tanh"), r + 1)
                    v.scalar_tensor_tensor(zg, zg, 1.0, acc[1][:, :, :], ALU.add, ALU.mult).then_inc(sem("z_read"), 1)
                if j == 6:
                    v.wait_ge(sem("x_back"), r + 1)
                    for t in range(TT):
                        v.tensor_tensor(heads(xdt[:, t, :]), heads(aux[1][:, t, :]), by_head(dt[:, t, :], r), ALU.mult)
                if j == 7:
                    v.wait_ge(sem("dskip_in"), 16)
                    for t in range(TT):
                        ins = v.tensor_tensor(heads(gbuf[:, t, :]), heads(aux[1][:, t, :]), by_head(dskip[:, :], r), ALU.mult)
                    ins.then_inc(sem("xdt_made"), 1)
                if j == 11:
                    v.wait_ge(sem("y_ready"), r + 1)
                    v.tensor_tensor(gbuf, aux[1][:, :, :], gbuf, ALU.add).then_inc(sem("y_read"), 1)
                if j == 12:
                    v.wait_ge(sem("y_read"), r + 1)
                    for t in range(TT):
                        ins = v.scalar_tensor_tensor(gbuf[:, t, :], gbuf[:, t, :], x_rs[:, t:t + 1], zg[:, t, :], ALU.mult, ALU.mult)
                    ins.then_inc(sem("gated"), 1)
                if j == 13:
                    v.wait_ge(sem("g_squared"), r + 1)
                    mean_eps(g_ms, g_ss, GC, 4 * EPS).then_inc(sem("g_ms"), 1)
                if j == end:
                    v.wait_ge(sem("gate_hi"), r + 1)
                    split_lo(aux[0], r * 4 + RB, r * 4 + N_OUT).then_inc(sem("gate_lo"), 1)

            def group(g, first):
                pos = Pos(IN0, g, PER_GROUP)
                for j in range(PER_GROUP):
                    lo(pos, j)
                    if not first:
                        tail(j, g - 1, 19)
                    if j == 9:
                        v.wait_ge(sem("bc_tap"), g + 1)
                        conv([(bct[:, i, :], aux[0][:, 0, i * SEQ:(i + 1) * SEQ], g + (INNER // P + i * GROUPS))
                              for i in range(2)])[1].then_inc(sem("bc_conv_lin"), 1)
                    if j == 10:
                        v.wait_ge(sem("bc_tanh"), g + 1)
                        v.scalar_tensor_tensor(bct, th, 1.0, bct, ALU.add, ALU.mult).then_inc(sem("bc_conv"), 1)
                    if j in (17, 18):
                        conv_x(g, 2 * (j - 17))
                    if first:
                        start(j)

            group(0, True)
            GROUP_LINKS = 12
            with v.Fori(1, GROUPS) as g:
                link.enter(g, 1, GROUP_LINKS)
                group(g, False)
                link.leave(GROUPS - 1)

            def add_resid(n, pos, last, scaled):
                v.wait_ge(sem("w_used"), pos.done(last))
                hb = h[:, :, n * NB:(n + 1) * NB]
                ps = acc[n % 2]
                if not scaled:
                    v.tensor_tensor(hb, ps[:, :, :], hb, ALU.add).then_inc(sem("resid_added"), 1)
                    return
                for t in range(TT):
                    ins = v.scalar_tensor_tensor(hb[:, t], ps[:, t, :], h_rs[:, t:t + 1], hb[:, t], ALU.mult, ALU.add)
                ins.then_inc(sem("resid_added"), 1)

            def resid_lo(n, turned, targets):
                v.wait_ge(sem("turned_hi"), turned)
                for region, w in targets:
                    ins = split_lo(aux[n % 2], region + 4 * n, w + 4 * n)
                ins.then_inc(sem("turned_lo"), 1)

            def resid_ms(squared):
                v.wait_ge(sem("h_squared"), squared)
                link(v.tensor_reduce(h_ms, h_ss.rearrange("p (t n) -> p t n", t=TT), AX.X, ALU.add))
                return mean_eps(h_ms, h_ms, D, EPS)

            to_mlp0, to_att, to_mlp1 = [(RA, N_MLP0)], [(RA, N_KV), (RC, N_ATT)], [(RA, N_MLP1)]

            for n in range(4):
                for j in range(16):
                    lo(Pos(OUT0), 16 * n + j)
                    if n == 0:
                        tail(j, GROUPS - 1, 15)
                    if n >= 1 and j == 2:
                        add_resid(n - 1, Pos(OUT0), 16 * n - 1, False)
                    if n >= 1 and j == 5:
                        resid_lo(n - 1, T_OUT + n, to_mlp0)

            def mlp(base, R, T, U, T_carry, before, after, prev, squared):
                def square(c, u):
                    v.wait_ge(sem("relu_made"), c * 4 + (U + u + 1))
                    v.scalar_tensor_tensor(act, acc[u % 2][:, :, :], 0.0, act, ALU.max, ALU.mult).then_inc(sem("up_read"), 1)

                def up_lo(c, u):
                    v.wait_ge(sem("turned_hi"), c * 4 + (T + u + 1))
                    v.tensor_tensor(st[:, RB + 4 * u:RB + 4 * u + 4, 1, :], whole(aux[u % 2]),
                                    st[:, RB + 4 * u:RB + 4 * u + 4, 0, :].bitcast(F32), ALU.subtract).then_inc(sem("turned_lo"), 1)

                def run(c, off, steps):
                    for j in range(8):
                        lo(Pos(base, c, PER_CHUNK), off + j)
                        steps(j)

                def after_up(c, u):
                    def steps(j):
                        if j == 2:
                            square(c, u)
                        if j == 5:
                            up_lo(c, u)
                    return steps

                def after_down(c, d, carry):
                    def steps(j):
                        if j == 2:
                            add_resid(d, Pos(base, c, PER_CHUNK), 32 + 8 * d + 7, True)
                        if j == 5 and carry:
                            resid_lo(d, T_carry + d + 1, after)
                    return steps

                def start(j):
                    if j == 2:
                        prev()
                    if j == 5:
                        resid_lo(3, T, before)
                    if j == 6:
                        link(resid_ms(squared))
                        link(v.reciprocal(h_rs, h_ms))

                run(0, 0, start)
                with v.Fori(0, 3) as c:
                    for u in range(1, 5):
                        run(c, 8 * u, after_up(c, u - 1))
                    for d in range(1, 5):
                        run(c, 32 + 8 * d, after_down(c, d - 1, False))
                for u in range(1, 5):
                    run(3, 8 * u, after_up(3, u - 1))
                for d in range(1, 4):
                    run(3, 32 + 8 * d, after_down(3, d - 1, after is not None))

            mlp(UP0, R_MLP0, T_MLP0, 0, T_MLP0_END, to_mlp0, to_att,
                lambda: add_resid(3, Pos(OUT0), 63, False), 4)

            def norm_sums(r, read):
                v.wait_ge(sem(read), r + 1)
                segs = lambda ap: ap.rearrange("p t (s c) -> p (t s) c", c=HD)
                link(v.tensor_tensor(act, kq, kq, ALU.mult))
                link(v.tensor_reduce(kq_ss, segs(act), AX.X, ALU.add))
                mean_eps(kq_ss, kq_ss, HD, EPS).then_inc(sem("kq_ms"), 1)

            def normalise(count, signal):
                v.wait_ge(sem("kq_rstd"), count)
                kqs = kq.rearrange("p t (s c) -> p (t s) c", c=HD)
                v.tensor_tensor(kqs, kqs, kq_rs.unsqueeze(2).to_broadcast([P, 8, HD]), ALU.mult).then_inc(sem(signal), 1)

            def maxima(r, t):
                if t == 0:
                    v.wait_ge(sem("sa_ready"), r + 1)
                    link(v.tensor_tensor(s0, aux[1][:, 0, :].rearrange("p (s k) -> p s k", s=4), mask0.unsqueeze(1).to_broadcast([P, 4, P]), ALU.add))
                    link(v.tensor_reduce(kq_ss[:, 0:4], s0, AX.X, ALU.max))
                else:
                    m = mask1.unsqueeze(1).to_broadcast([P, 2, SEQ])
                    v.tensor_tensor(s1[:, 0:2, :], aux[1][:, 1, :].rearrange("p (s k) -> p s k", s=2), m, ALU.add)
                    v.wait_ge(sem("sb_ready"), r + 1)
                    link(v.tensor_tensor(s1[:, 2:4, :], aux[0][:, 0, :].rearrange("p (s k) -> p s k", s=2), m, ALU.add))
                    link(v.tensor_reduce(kq_ss[:, 4:8], s1, AX.X, ALU.max))
                c = kq_ss[:, 4 * t:4 * t + 4]
                v.tensor_scalar(c, c, -(HD ** -0.5), None, ALU.mult).then_inc(sem("max_made"), 1)

            def combine(r):
                v.wait_ge(sem("exp_made"), 2 * (r + 1))
                link(v.reciprocal(kq_rs, kq_rs))
                link(v.tensor_tensor(kq_rs, kq_rs, coef, ALU.mult))
                each = [(sc, k, t * 4 + 2 * k) for k in range(2) for t, sc in enumerate((s0, s1))]
                scaled = [link.count(v.tensor_scalar(sc[:, 2 * k + 1, :], sc[:, 2 * k + 1, :], kq_rs[:, n + 1:n + 2], None, ALU.mult))
                          for sc, k, n in each]
                for (sc, k, n), made in zip(each, scaled):
                    link.after(made)
                    ins = v.scalar_tensor_tensor(sc[:, 2 * k, :], sc[:, 2 * k, :], kq_rs[:, n:n + 1], sc[:, 2 * k + 1, :], ALU.mult, ALU.add)
                ins.then_inc(sem("p_made"), 1)

            def o_means(r):
                v.wait_ge(sem("o_squared"), r + 1)
                mean_eps(o_ss, o_ss, 2 * HD, EPS).then_inc(sem("o_ms"), 1)

            def o_lo(r):
                v.wait_ge(sem("o_hi"), r + 1)
                for i in range(4):
                    kt = r * 4 + (RB + i)
                    ins = v.scalar_tensor_tensor(one_tile(st, kt, 1), turned_tile(aux[0], i), param(N_SUB + i % 2),
                                                 one_tile(st, kt, 0).bitcast(F32), ALU.mult, ALU.subtract)
                ins.then_inc(sem("o_lo"), 1)

            def pair(j, first):
                pos = Pos(ATT0, j, PER_PAIR)
                for i in range(PER_PAIR):
                    lo(pos, i)
                    if first and i == 2:
                        add_resid(3, Pos(UP0, 3, PER_CHUNK), PER_CHUNK - 1, True)
                    if first and i == 5:
                        resid_lo(3, T_MLP0_END + 4, to_att)
                    if first and i == 6:
                        resid_ms(8).then_inc(sem("h_ms"), 1)
                    if not first:
                        r = j - 1
                        if i == 4:
                            norm_sums(r, "q_read")
                        if i == 5:
                            normalise(r * 2 + 2, "q_normed")
                        if i == 12:
                            maxima(r, 0)
                        if i == 13:
                            maxima(r, 1)
                        if i == 16:
                            combine(r)
                    if i == 20:
                        if not first:
                            v.wait_ge(sem("o_ready"), j)
                        norm_sums(j, "k_read")
                    if i == 21:
                        normalise(j * 2 + 1, "k_normed")
                    if not first:
                        if i == 20:
                            o_means(r)
                        if i == 23:
                            o_lo(r)

            pair(0, True)
            PAIR_LINKS = 14
            with v.Fori(1, 4) as j:
                link.enter(j, 1, PAIR_LINKS)
                pair(j, False)
                link.leave(3)

            for i in range(len(WO_ORDER)):
                lo(Pos(WO0), i)
                if i == 2:
                    norm_sums(3, "q_read")
                if i == 3:
                    normalise(8, "q_normed")
                if i == 7:
                    maxima(3, 0)
                    maxima(3, 1)
                if i == 8:
                    combine(3)
                if i == 12:
                    o_means(3)
                if i == 13:
                    o_lo(3)
                for n, last, at_add, at_lo in ((0, 13, 16, 20), (1, 15, 18, 22), (2, 23, 26, 29)):
                    if i == at_add:
                        add_resid(n, Pos(WO0), last, False)
                    if i == at_lo:
                        resid_lo(n, T_WO + n + 1, to_mlp1)

            mlp(UP1, R_MLP1, T_MLP1, 16, None, to_mlp1, None,
                lambda: add_resid(3, Pos(WO0), 31, False), 12)
            v.wait_ge(sem("w_used"), PIECES)
            for t in range(TT):
                last = h[:, t, 3 * NB:]
                v.scalar_tensor_tensor(last, acc[1][:, t, :], h_rs[:, t:t + 1], last, ALU.mult, ALU.add).then_inc(sem("last_added"), 1)

        @block.gpsimd
        def _(gp):
            link = Chain(gp, sem("gp_chain"))

            def keep(ap, pattern, base, mult, fill, then=None, op=ALU.is_ge):
                ins = gp.affine_select(out=ap, in_=ap, compare_op=op, fill=fill, base=base, pattern=pattern, channel_multiplier=mult)
                if then:
                    ins.then_inc(sem(then), 1)
                else:
                    link(ins)

            def rsqrt(out, in_, signal):
                gp.tensor_tensor(out, in_, nhalf[:, 0:out.shape[1]], ALU.pow).then_inc(sem(signal), 1)

            link(gp.memset(nhalf, -0.5))
            gp.memset(ident[:, :], 0.0).then_inc(sem("ident_made"), 1)
            gp.wait_ge(sem("ident_made"), 1)
            keep(ident[:, :], [[-1, P]], 0, 1, 1.0, "ident_made", ALU.not_equal)
            for i, v in enumerate((lam_q1, lam_k1, lam_q2, lam_k2)):
                gp.dma_start(lamv[:, i, :], v.to_broadcast([P, HD])).then_inc(sem("lam_in"), 16)
            gp.dma_start(alog, ssm_a_log.to_broadcast([P, HEADS])).then_inc(sem("alog_in"), 16)
            gp.dma_start(dskip[:, :], ssm_d.to_broadcast([P, HEADS])).then_inc(sem("dskip_in"), 16)
            c = 5 * KT + INNER // P
            for w, n in ((k_norm_w, 1), (q_norm_w[0], 1), (subln_w[0], 2)):
                gp.dma_start(prow[c:c + n, 3, :], w.rearrange("(r c) -> r c", c=P)).then_inc(sem("head_rows_in"), 16)
                c += n
            km = lambda i: kmat[:, i, :]
            gp.memset(kmat[:, 2:5, :], 1.0)
            gp.memset(kmat[:, 1, 0:CH], 1.0)
            gp.memset(kmat[:, 1, CH:], -1.0)
            gp.memset(kmat[:, 0, 0:CH], -1.0)
            link(gp.memset(kmat[:, 0, CH:], 0.0))
            keep(kmat[:, 0, 0:CH], [[1, CH]], 0, -1, 0.0)
            keep(kmat[:, 1, 0:CH], [[-1, CH]], -1, 1, 0.0)
            keep(kmat[:, 1, 0:CH], [[0, CH]], CH - 1, -1, 0.0)
            keep(kmat[:, 1, CH:], [[1, CH]], CH, -1, 0.0)
            keep(kmat[:, 1, CH:], [[0, CH]], -CH, 1, 0.0)
            keep(km(2), [[-1, P]], -1, 1, 0.0)
            keep(km(3), [[0, P]], CH - 1, -1, 0.0)
            keep(kmat[:, 4, CH:], [[0, CH]], -CH, 1, 0.0)
            keep(km(4), [[1, P]], 0, -1, 0.0, "kmat_made")
            link(gp.memset(no_later[:, :], 0.0))
            keep(no_later[:, :], [[1, P]], 0, -1, NEG)
            gp.wait_ge(sem("x_ms"), 1)
            rsqrt(x_rs, x_ss, "x_rstd")
            gp.wait_ge(sem("rows_made"), 1)
            gp.dma_start(rows_dram, rowsb[0:HEADS, :]).then_inc(sem("rows_out"), 16)
            gp.wait_ge(sem("rows_out"), 16)

            def rows_of(g):
                src = rows_dram[one(g * HG, HG), :]
                gp.dma_start(m0, src.unsqueeze(0).to_broadcast([P, HG, SEQ])).then_inc(sem("row_in"), 16)

            def gate_rstd(r):
                gp.wait_ge(sem("g_ms"), r + 1)
                rsqrt(g_rs, g_ms, "g_rstd")

            def exponents(g, first):
                gp.wait_ge(sem("row_in"), g * 16 + 16)
                colp = lambda n0, n: cols3(colv, n0, n, g * HG).rearrange("p c h -> p h c").unsqueeze(3).to_broadcast([P, HG, n, CH])
                lch = lambda ap, n: ap.rearrange("p h (c l) -> p h c l", c=n)
                later = no_later[:, :].unsqueeze(1).to_broadcast([P, HG, P])
                gp.tensor_tensor(lch(m1, 2), lch(m0[:, :, P:], 2), colp(4, 2), ALU.add).then_inc(sem("exponents"), 1)
                gp.wait_ge(sem("exponents"), g * 2 + 1)
                gp.tensor_tensor(m1, m1, later, ALU.add).then_inc(sem("masked"), 1)
                if not first:
                    gate_rstd(g - 1)
                gp.tensor_tensor(lch(m0, 4), lch(m0, 4), colp(0, 4), ALU.add).then_inc(sem("exponents"), 1)
                gp.wait_ge(sem("exponents"), g * 2 + 2)
                gp.tensor_tensor(m0[:, :, 0:P], m0[:, :, 0:P], later, ALU.add).then_inc(sem("masked"), 1)

            def times_cb(g):
                gp.wait_ge(sem("cb_read"), g + 1)
                for i, (m, c) in enumerate(((m1, cb[:, SEQ:]), (m0, cb[:, 0:SEQ]))):
                    gp.wait_ge(sem("decay_made"), g * 2 + (i + 1))
                    gp.tensor_tensor(m, m, c.unsqueeze(1).to_broadcast([P, HG, c.shape[1]]), ALU.mult).then_inc(sem("m_made"), 1)

            gp.wait_ge(sem("decays_read"), 1)
            rows_of(0)
            exponents(0, True)
            times_cb(0)
            with gp.Fori(1, GROUPS) as g:
                gp.wait_ge(sem("y_ready"), g)
                rows_of(g)
                exponents(g, False)
                times_cb(g)
            gate_rstd(GROUPS - 1)

            gp.wait_ge(sem("resid_added"), 1)
            gp.memset(mask0, 0.0)
            link(gp.memset(mask1, 0.0))
            keep(mask0[:, CH:], [[0, CH]], -CH, 1, NEG)
            keep(mask1[:, 3 * CH:], [[0, CH]], -CH, 1, NEG, "masks_made")

            gp.wait_ge(sem("masks_made"), 1)
            gp.wait_ge(sem("h_ms"), 1)
            rsqrt(h_rs, h_ms, "h_rstd")

            def kq_rstd(count):
                gp.wait_ge(sem("kq_ms"), count)
                rsqrt(kq_rs, kq_ss, "kq_rstd")

            kq_rstd(1)
            with gp.Fori(1, 4) as j:
                kq_rstd(j * 2)
                kq_rstd(j * 2 + 1)
                gp.wait_ge(sem("o_ms"), j)
                rsqrt(o_rs, o_ss, "o_rstd")
            kq_rstd(8)
            gp.wait_ge(sem("o_ms"), 4)
            rsqrt(o_rs, o_ss, "o_rstd")


_INS = ["x", "mlp_norm_w", "w_up", "w_down", "ssm_norm_w", "ssm_w_in", "ssm_conv_w", "ssm_conv_b", "ssm_dt_bias",
        "ssm_a_log", "ssm_d", "ssm_out_norm_w", "ssm_w_out", "kv_norm_w", "w_kv", "k_norm_w", "attn_norm_w", "w_q",
        "q_norm_w", "lam_q1", "lam_k1", "lam_q2", "lam_k2", "subln_w", "w_o"]


def kernel(**inputs):
    import concourse.bacc as bacc
    from concourse.bass_utils import run_bass_kernel_spmd

    nc = bacc.Bacc("TRN2", target_bir_lowering=False, num_devices=1)
    arrays, args = {}, []
    for name in _INS:
        a = np.ascontiguousarray(inputs[name])
        arrays[f"in_{name}"] = a
        args.append(nc.dram_tensor(f"in_{name}", a.shape, mybir.dt.from_np(a.dtype), kind="ExternalInput").ap())
    args.append(nc.dram_tensor("out_0", (1, SEQ, D), F32, kind="ExternalOutput").ap())
    trunk(nc, *args)
    r = run_bass_kernel_spmd(nc, [arrays], core_ids=[0])
    return r.results[0]["out_0"]
```
